# Optimizing a Trainium2 kernel written in Bass

```python
import math
import jax
import jax.numpy as jnp
from jax import lax
import numpy as np

D_MODEL = 1024
BATCH = 1
SEQ = 1024
DEPTH = 2
DEC_BATCH = 1
DEC_SEQ = 32
PAST_LEN = 1024

CHUNK = 64
QBLOCK = 128
D_MIX = D_MODEL
M_HEADS = 8
M_DK = 64
M_DV = 64
M_WIDTH = M_HEADS * M_DV
A_HEADS = 8
NOPE_DIM = 64
ROPE_DIM = 32
V_DIM = 64
A_WIDTH = A_HEADS * V_DIM
Q_RANK = 256
KV_RANK = 256
ROPE_THETA = 10000.0
D_FF = -(-8 * D_MODEL // (3 * 256)) * 256
RMS_EPS = 1e-6
F_BIAS_INIT = 3.0
ATTN_SCALE = (NOPE_DIM + ROPE_DIM) ** -0.5
IN_SIZES = (M_HEADS * M_DK, M_HEADS * M_DK, M_WIDTH, M_WIDTH, 2 * M_HEADS, Q_RANK, KV_RANK, ROPE_DIM)
D_IN = 2 * M_HEADS * M_DK + 2 * M_WIDTH + 2 * M_HEADS + Q_RANK + KV_RANK + ROPE_DIM

kernel_name = "hymba_mlstm_mla_streaming_step"

def rmsnorm(x, g):
    xf = x.astype(jnp.float32)
    y = xf * lax.rsqrt(jnp.mean(xf * xf, axis=-1, keepdims=True) + RMS_EPS)
    return (y * g.astype(jnp.float32)).astype(x.dtype)

def apply_rope(x, pos):
    half = ROPE_DIM // 2
    inv = ROPE_THETA ** (-jnp.arange(half, dtype=jnp.float32) / half)
    ang = pos.astype(jnp.float32)[:, None] * inv[None, :]
    shape = (ang.shape[0],) + (1,) * (x.ndim - 3) + (half,)
    cos = jnp.cos(ang).reshape(shape)
    sin = jnp.sin(ang).reshape(shape)
    x1 = x[..., :half].astype(jnp.float32)
    x2 = x[..., half:].astype(jnp.float32)
    return jnp.concatenate([x1 * cos - x2 * sin, x1 * sin + x2 * cos], axis=-1).astype(x.dtype)

def project_inputs(h, pos, w_in, b_gates, g_q_norm, w_uq, g_kv_norm):
    B, S, _ = h.shape
    idx = [int(i) for i in np.cumsum(IN_SIZES)[:-1]]
    qm, km, vm, om, gates, cq, ckv, kr = jnp.split(h @ w_in, idx, axis=-1)
    qm = qm.reshape(B, S, M_HEADS, M_DK)
    km = km.reshape(B, S, M_HEADS, M_DK) * (M_DK ** -0.5)
    vm = vm.reshape(B, S, M_HEADS, M_DV)
    gates = gates.astype(jnp.float32) + b_gates.astype(jnp.float32)
    ig = gates[..., :M_HEADS]
    lf = jax.nn.log_sigmoid(gates[..., M_HEADS:])
    q = (rmsnorm(cq, g_q_norm) @ w_uq).reshape(B, S, A_HEADS, NOPE_DIM + ROPE_DIM)
    q_nope = q[..., :NOPE_DIM]
    q_rope = apply_rope(q[..., NOPE_DIM:], pos)
    ckv = rmsnorm(ckv, g_kv_norm)
    kr = apply_rope(kr, pos)
    return qm, km, vm, om, ig, lf, q_nope, q_rope, ckv, kr

def expand_kv(ckv, w_ukv):
    B, T, _ = ckv.shape
    kv = (ckv @ w_ukv).reshape(B, T, A_HEADS, NOPE_DIM + V_DIM)
    return kv[..., :NOPE_DIM], kv[..., NOPE_DIM:]

def mlstm_chunk(carry, xs):
    C0, n0, m0 = carry
    q, k, v, ig, lf = xs
    q = q.astype(jnp.float32)
    k = k.astype(jnp.float32)
    v = v.astype(jnp.float32)
    L = q.shape[2]
    b = jnp.cumsum(lf, axis=-1)
    causal = jnp.tril(jnp.ones((L, L), dtype=bool))
    D = jnp.where(causal, b[..., :, None] - b[..., None, :] + ig[..., None, :], -jnp.inf)
    inter = b + m0[..., None]
    m = jnp.maximum(inter, jnp.max(D, axis=-1))
    S = jnp.einsum('bhtd,bhsd->bhts', q, k) * jnp.exp(D - m[..., None])
    w_inter = jnp.exp(inter - m)
    num = w_inter[..., None] * jnp.einsum('bhtd,bhde->bhte', q, C0) + jnp.einsum('bhts,bhse->bhte', S, v)
    den = w_inter * jnp.einsum('bhtd,bhd->bht', q, n0) + jnp.sum(S, axis=-1)
    h = num / jnp.maximum(jnp.abs(den), jnp.exp(-m))[..., None]
    m_new = m[..., -1]
    w = jnp.exp(b[..., -1:] - b + ig - m_new[..., None])
    decay = jnp.exp(b[..., -1] + m0 - m_new)
    C_new = decay[..., None, None] * C0 + jnp.einsum('bhs,bhsd,bhse->bhde', w, k, v)
    n_new = decay[..., None] * n0 + jnp.einsum('bhs,bhsd->bhd', w, k)
    return (C_new, n_new, m_new), h

def mlstm_prompt(qm, km, vm, ig, lf):
    B, S, H, _ = qm.shape
    nc = S // CHUNK

    def blocks4(t):
        return t.reshape(B, nc, CHUNK, H, t.shape[-1]).transpose(1, 0, 3, 2, 4)

    def blocks3(t):
        return t.reshape(B, nc, CHUNK, H).transpose(1, 0, 3, 2)

    init = (jnp.zeros((B, H, M_DK, M_DV), jnp.float32),
            jnp.zeros((B, H, M_DK), jnp.float32),
            jnp.zeros((B, H), jnp.float32))
    carry, hs = lax.scan(mlstm_chunk, init,
                         (blocks4(qm), blocks4(km), blocks4(vm), blocks3(ig), blocks3(lf)))
    hs = hs.transpose(1, 2, 0, 3, 4).reshape(B, H, S, M_DV)
    return carry, hs

def mlstm_sample(state, qm, km, vm, ig, lf):
    return mlstm_chunk(state, (qm.transpose(0, 2, 1, 3), km.transpose(0, 2, 1, 3), vm.transpose(0, 2, 1, 3),
                               ig.transpose(0, 2, 1), lf.transpose(0, 2, 1)))

def mlstm_output(h_cell, om, g_head, dtype):
    B, H, S, _ = h_cell.shape
    h = h_cell.transpose(0, 2, 1, 3)
    h = h * lax.rsqrt(jnp.mean(h * h, axis=-1, keepdims=True) + RMS_EPS)
    h = h * g_head.astype(jnp.float32).reshape(M_HEADS, M_DV)
    o = jax.nn.sigmoid(om.astype(jnp.float32)).reshape(B, S, M_HEADS, M_DV)
    return (o * h).reshape(B, S, M_WIDTH).astype(dtype)

def mla_attend(qn, qr, kn, kr, v, mask):
    s = (jnp.einsum('bqhd,bkhd->bhqk', qn, kn) + jnp.einsum('bqhd,bkd->bhqk', qr, kr)).astype(jnp.float32)
    s = s * ATTN_SCALE
    if mask is not None:
        s = jnp.where(mask, s, -jnp.inf)
    p = jax.nn.softmax(s, axis=-1).astype(v.dtype)
    return jnp.einsum('bhqk,bkhd->bqhd', p, v)

def mla_prompt_attention(q_nope, q_rope, k_nope, k_rope, v):
    B, S, H, _ = q_nope.shape
    nb = S // QBLOCK
    qn = q_nope.reshape(B, nb, QBLOCK, H, NOPE_DIM).transpose(1, 0, 2, 3, 4)
    qr = q_rope.reshape(B, nb, QBLOCK, H, ROPE_DIM).transpose(1, 0, 2, 3, 4)
    kpos = jnp.arange(S)

    def block(args):
        i, qn_b, qr_b = args
        qpos = i * QBLOCK + jnp.arange(QBLOCK)
        reach = (qpos // CHUNK + 1) * CHUNK
        mask = kpos[None, :] < reach[:, None]
        return mla_attend(qn_b, qr_b, k_nope, k_rope, v, mask)

    out = lax.map(block, (jnp.arange(nb), qn, qr))
    return out.transpose(1, 0, 2, 3, 4).reshape(B, S, A_WIDTH)

def residual_update(x, h_m, attn, w_out, g_post_mix, g_pre_ffn, w_ffn_in, w_ffn_out, g_post_ffn):
    x = x + rmsnorm(jnp.concatenate([h_m, attn], axis=-1) @ w_out, g_post_mix)
    h = rmsnorm(x, g_pre_ffn)
    gate, up = jnp.split(h @ w_ffn_in, 2, axis=-1)
    return x + rmsnorm((jax.nn.silu(gate) * up) @ w_ffn_out, g_post_ffn)

def setup_inputs(seed: int = 0) -> dict:
    key = jax.random.key(seed)
    ks = jax.random.split(key, 24)
    f32 = jnp.float32

    def nrm(k, shape, scale):
        return jax.random.normal(k, shape, f32) * scale

    def gain(k, shape):
        return 1.0 + 0.05 * jax.random.normal(k, shape, f32)

    b_gates = jnp.concatenate([nrm(ks[8], (DEPTH, M_HEADS), 0.1),
                               F_BIAS_INIT + nrm(ks[9], (DEPTH, M_HEADS), 0.5)], axis=-1)
    return {
        "x_prompt": nrm(ks[0], (BATCH, SEQ, D_MODEL), 1.0),
        "x_sample": nrm(ks[1], (DEC_BATCH, DEC_SEQ, D_MODEL), 1.0),
        "cache_ckv": nrm(ks[2], (DEPTH, DEC_BATCH, PAST_LEN, KV_RANK), 1.0),
        "cache_krope": nrm(ks[3], (DEPTH, DEC_BATCH, PAST_LEN, ROPE_DIM), 1.0),
        "state_mlstm_C": nrm(ks[4], (DEPTH, DEC_BATCH, M_HEADS, M_DK, M_DV), 0.5),
        "state_mlstm_n": nrm(ks[5], (DEPTH, DEC_BATCH, M_HEADS, M_DK), 0.5),
        "state_mlstm_m": nrm(ks[6], (DEPTH, DEC_BATCH, M_HEADS), 1.0),
        "g_pre_mix": gain(ks[10], (DEPTH, D_MODEL)),
        "g_post_mix": gain(ks[11], (DEPTH, D_MODEL)),
        "g_pre_ffn": gain(ks[12], (DEPTH, D_MODEL)),
        "g_post_ffn": gain(ks[13], (DEPTH, D_MODEL)),
        "w_in": nrm(ks[7], (DEPTH, D_MODEL, D_IN), D_MODEL ** -0.5),
        "b_gates": b_gates,
        "g_mlstm_head": gain(ks[14], (DEPTH, M_WIDTH)),
        "g_q_norm": gain(ks[15], (DEPTH, Q_RANK)),
        "w_uq": nrm(ks[16], (DEPTH, Q_RANK, A_HEADS * (NOPE_DIM + ROPE_DIM)), Q_RANK ** -0.5),
        "g_kv_norm": gain(ks[17], (DEPTH, KV_RANK)),
        "w_ukv": nrm(ks[18], (DEPTH, KV_RANK, A_HEADS * (NOPE_DIM + V_DIM)), KV_RANK ** -0.5),
        "w_out": nrm(ks[19], (DEPTH, D_MIX, D_MODEL), D_MIX ** -0.5),
        "w_ffn_in": nrm(ks[20], (DEPTH, D_MODEL, 2 * D_FF), D_MODEL ** -0.5),
        "w_ffn_out": nrm(ks[21], (DEPTH, D_FF, D_MODEL), D_FF ** -0.5),
    }

def reference(x_prompt, x_sample, cache_ckv, cache_krope, state_mlstm_C, state_mlstm_n, state_mlstm_m,
              g_pre_mix, g_post_mix, g_pre_ffn, g_post_ffn, w_in, b_gates, g_mlstm_head,
              g_q_norm, w_uq, g_kv_norm, w_ukv, w_out, w_ffn_in, w_ffn_out):
    pos_p = jnp.arange(x_prompt.shape[1])
    pos_s = cache_ckv.shape[2] + jnp.arange(x_sample.shape[1])
    xp, xs = x_prompt, x_sample
    ckv_p, kr_p, C_p, n_p, m_p = [], [], [], [], []
    ckv_s, kr_s, C_s, n_s, m_s = [], [], [], [], []
    for l in range(DEPTH):
        h = rmsnorm(xp, g_pre_mix[l])
        qm, km, vm, om, ig, lf, qn, qr, ckv, kr = project_inputs(
            h, pos_p, w_in[l], b_gates[l], g_q_norm[l], w_uq[l], g_kv_norm[l])
        (C, n, m), hcell = mlstm_prompt(qm, km, vm, ig, lf)
        kn, v = expand_kv(ckv, w_ukv[l])
        attn = mla_prompt_attention(qn, qr, kn, kr, v)
        xp = residual_update(xp, mlstm_output(hcell, om, g_mlstm_head[l], xp.dtype), attn, w_out[l],
                             g_post_mix[l], g_pre_ffn[l], w_ffn_in[l], w_ffn_out[l], g_post_ffn[l])
        ckv_p.append(ckv)
        kr_p.append(kr)
        C_p.append(C)
        n_p.append(n)
        m_p.append(m)
        h = rmsnorm(xs, g_pre_mix[l])
        qm, km, vm, om, ig, lf, qn, qr, ckv, kr = project_inputs(
            h, pos_s, w_in[l], b_gates[l], g_q_norm[l], w_uq[l], g_kv_norm[l])
        state = (state_mlstm_C[l].astype(jnp.float32), state_mlstm_n[l].astype(jnp.float32),
                 state_mlstm_m[l].astype(jnp.float32))
        (C, n, m), hcell = mlstm_sample(state, qm, km, vm, ig, lf)
        ckv_all = jnp.concatenate([cache_ckv[l], ckv], axis=1)
        kr_all = jnp.concatenate([cache_krope[l], kr], axis=1)
        kn, v = expand_kv(ckv_all, w_ukv[l])
        Bs, T = xs.shape[0], xs.shape[1]
        attn = mla_attend(qn, qr, kn, kr_all, v, None).reshape(Bs, T, A_WIDTH)
        xs = residual_update(xs, mlstm_output(hcell, om, g_mlstm_head[l], xs.dtype), attn, w_out[l],
                             g_post_mix[l], g_pre_ffn[l], w_ffn_in[l], w_ffn_out[l], g_post_ffn[l])
        ckv_s.append(ckv)
        kr_s.append(kr)
        C_s.append(C)
        n_s.append(n)
        m_s.append(m)
    return (xp, xs,
            jnp.stack(ckv_p), jnp.stack(kr_p), jnp.stack(C_p), jnp.stack(n_p), jnp.stack(m_p),
            jnp.stack(ckv_s), jnp.stack(kr_s), jnp.stack(C_s), jnp.stack(n_s), jnp.stack(m_s))


_drawn_inputs = setup_inputs


def setup_inputs(seed=0):
    import zlib

    import numpy as np

    out = dict(_drawn_inputs(seed))
    spreads = {}
    factors = {'g_q_norm': 4.183}
    for name, (base, spread) in spreads.items():
        noise = np.random.default_rng([zlib.crc32(name.encode()), seed]).standard_normal(out[name].shape)
        drawn = base * np.exp(spread * noise) if base else spread * noise
        out[name] = jnp.asarray(drawn.astype(out[name].dtype))
    for name, factor in factors.items():
        out[name] = (out[name] * factor).astype(out[name].dtype)
    return out
```

```python
from contextlib import ExitStack

import concourse.bass as bass
from concourse import mybir

F32 = mybir.dt.float32
F32R = mybir.dt.float32r
ALU = mybir.AluOpType
ACT = mybir.ActivationFunctionType
AX = mybir.AxisListType.X

P = 128
D = 1024
KT = D // P
SEQ, DEC, PAST = 1024, 32, 1024
T = SEQ + DEC
NG = 3
TG = T // NG
LAYERS = 2
HEADS, HD = 8, 64
PAIRS = HEADS // 2
ROPE = 32
RANK = 256
DFF = 2816
FT = DFF // P
FG = FT // 2
CH = 9
TP = CH * P
CG = 3
KEYS = T + PAST
HB = HD + 1
SLAB = 1024
BANK = 512
EPS = 1e-6
SCALE = float(96) ** -0.5
NEG = -1e30

COL_Q, COL_K, COL_V, COL_O, COL_G = 0, 512, 1024, 1536, 2048
COL_CQ, COL_CKV, COL_KR = 2064, 2320, 2576

SLOT_PAIRS, SLOT_LATENT = (1, 0), (9, 8)
SLOT_HEADS, SLOT_OUT, SLOT_FFN = (11, 10), (15, 10), (19, 14)
SLOT_USES = (52, 47)
PLAIN_0 = 47
SET_PAIRS, SET_LATENT, SET_OUT, SET_FFN = (1, 0), (9, 8), (11, 10), (15, 14)
SET_USES = (81, 80)
TILES = 161
TILE_PAIRS, TILE_LATENT, TILE_OUT, TILE_FFN = 1, 17, 21, 29
NORMS = 6
SUMS = 4 * (KT - 1)

BLOCKS = []
for _kt in range(SEQ // P):
    if _kt * P < 512:
        BLOCKS.append((_kt, _kt * P, 512))
    BLOCKS.append((_kt, max(512, _kt * P), SEQ))
NB = len(BLOCKS)


def encoder_step(nc, a, o):
    with ExitStack() as ctx:
        def sb(name, cols, dt=F32, rows=P):
            return ctx.enter_context(nc.sbuf_tensor(name, [rows, cols], dt))

        def sem(name):
            return ctx.enter_context(nc.semaphore(name))

        X = sb("residual", KT * T)
        Y = sb("branch", KT * T)
        HH, HL = sb("act_hi", KT * T, F32R), sb("act_lo", KT * T, F32R)
        RH, RL = sb("small_hi", 3104, F32R), sb("small_lo", 3104, F32R)
        RAW = sb("slab_raw", 2 * SLAB)
        SH, SL = sb("slab_hi", 2 * SLAB, F32R), sb("slab_lo", 2 * SLAB, F32R)
        W2 = sb("work", 2 * T)
        SS = sb("sum_squares", T)
        RS = sb("rstd", T)
        N4 = sb("gates_by_token", CH * 32)
        UROW = sb("b_minus_m", TP, rows=8)
        IDN = sb("identity", P)
        ONES = sb("ones", P)
        CM = sb("causal", P)
        CONST = sb("constants", 2)
        BM = sb("pair_mask", 2 * HB)
        GN = sb("gains", LAYERS * 4 * KT)
        GM = sb("gain_mlstm", LAYERS * PAIRS)
        GC = sb("gain_latent", LAYERS * 4)
        BG = sb("gate_bias", LAYERS * 3, rows=8)
        SEL = sb("pair_select", PAIRS * P, rows=8)
        DEC_ALL = sb("decay_by_pair", PAIRS * CH)
        SMALL = sb("small", 64)
        PS = ctx.enter_context(nc.psum_tensor("acc", [P, 8 * BANK], F32))
        x_spill = nc.dram_tensor("x_spill", [P, KT * T], F32, kind="Internal").ap()

        def bank(b, w, rows=(0, P), off=0):
            return PS[rows[0]:rows[1], b * BANK + off:b * BANK + off + w]

        def pset(s, rows=(0, P)):
            return PS[rows[0]:rows[1], 3 * s * BANK:3 * (s + 1) * BANK].rearrange("p (n c) -> p n c", n=3)[:, :, 0:TG]

        def by(ap, n):
            return ap.rearrange("p (n c) -> p n c", n=n)

        def xt(k):
            return X[:, k * T:(k + 1) * T]

        def yt(k):
            return Y[:, k * T:(k + 1) * T]

        QT, KTT, VT, OM = X[:, 0:TP], X[:, TP:2 * TP], X[:, 2 * TP:3 * TP], X[:, 3 * TP:3 * TP + T]
        KW = X[:, 4 * TP:5 * TP]
        VX = X[:, 5 * TP:5 * TP + CH * 2 * HB]
        C0 = 5 * TP + CH * 2 * HB
        CS = X[:, C0:C0 + 11 * 2 * HB]

        def cs(c, rows=(0, P), cols=(0, 2 * HB)):
            return X[rows[0]:rows[1], C0 + c * 2 * HB + cols[0]:C0 + c * 2 * HB + cols[1]]

        def gt(i, c0=0, c1=TP):
            return X[0:8, i * TP + c0:i * TP + c1]
        G4 = 5 * TP
        PT, WT = W2[:, 0:6 * P], W2[:, 6 * P:12 * P]
        T1, UM = W2[:, 12 * P:12 * P + 3 * 2 * HB], RS
        HBUF, SQ = SS[:, 0:3 * P], SS[:, 3 * P:6 * P]
        CQ, CKV, KTO = 0, 2 * T, 2 * T + 2 * KEYS
        QTO, VO, PO = 0, T, T + SEQ
        QF, VTF, VS, PF, PTS = 0, T, T + KEYS, T + KEYS + CH * HD, T + KEYS + CH * HD + 2 * BANK
        KRF, TRIG = 5280, 7360
        CACHE, STAGE = 4 * T, 4 * T + 8 * 288
        KRRAW = 7 * T

        const_loaded, x_loaded = sem("const_loaded"), sem("x_loaded")
        raw_landed = [sem("raw_landed0"), sem("raw_landed1")]
        gate_raw_landed, head_raw_landed = sem("gate_raw_landed"), sem("head_raw_landed")
        raw_free = [sem("raw_free0"), sem("raw_free1")]
        slab_ready = [sem("slab_ready0"), sem("slab_ready1")]
        slab_free = [sem("slab_free0"), sem("slab_free1")]
        tile_done = sem("tile_done")
        emptied = [sem("set_emptied0"), sem("set_emptied1")]
        x_ready, x_spilled, x_back = sem("x_ready"), sem("x_spilled"), sem("x_back")
        in_turned, in_taken = sem("in_turned"), sem("in_taken")
        sq_ready, sq_added = sem("sq_ready"), sem("sq_added")
        csq_ready, csq_added = sem("csq_ready"), sem("csq_added")
        ms_ready, rs_ready = sem("ms_ready"), sem("rs_ready")
        scaled, hi_ready, h_ready = sem("scaled"), sem("hi_ready"), sem("h_ready")
        f_ready, softplus_ready, args_ready = sem("f_ready"), sem("softplus_ready"), sem("args_ready")
        gate_exps, gate_turned, gates_ready = sem("gate_exps"), sem("gate_turned"), sem("gates_ready")
        m_stored = sem("m_stored")
        mixer_cleared = sem("mixer_cleared")
        state_loaded, state_stored, states_ready = sem("state_loaded"), sem("state_stored"), sem("states_ready")
        kv_turned, vx_ready, kw_ready, upd_ready = sem("kv_turned"), sem("vx_ready"), sem("kw_ready"), sem("upd_ready")
        um_ready, u_ready, dm_ready, pt_ready = sem("um_ready"), sem("u_ready"), sem("dm_ready"), sem("pt_ready")
        st_ready, w_ready, num_ready = sem("st_ready"), sem("w_ready"), sem("num_ready")
        ms_head, rr_ready, hn_ready, ht_ready = sem("ms_head"), sem("rr_ready"), sem("hn_ready"), sem("ht_ready")
        mout_done = sem("mout_done")
        trig_loaded, cache_loaded = sem("trig_loaded"), sem("cache_loaded")
        lat_scaled, lat_hi, lat_ready = sem("lat_scaled"), sem("lat_hi"), sem("lat_ready")
        krope_ready, cache_turned, cache_hi, cache_lo = sem("krope_ready"), sem("cache_turned"), sem("cache_hi"), sem("cache_lo")
        kr_turned, kr_full, krope_hi, keys_ready = sem("kr_turned"), sem("kr_full"), sem("krope_hi"), sem("keys_ready")
        nat_turned, nat_staged = sem("nat_turned"), sem("nat_staged")
        nat_stored = [sem(f"nat_stored{i}") for i in range(3)]
        q_proj, kv_proj, qnope_ready, qf_ready = sem("q_proj"), sem("kv_proj"), sem("qnope_ready"), sem("qf_ready")
        qhi_ready, qk_ready, khi_ready, vt_ready = sem("qhi_ready"), sem("qk_ready"), sem("khi_ready"), sem("vt_ready")
        v_turned, vhi_ready, v_ready = sem("v_turned"), sem("vhi_ready"), sem("v_ready")
        smax_ready, smax_taken, max_ready = sem("smax_ready"), sem("smax_taken"), sem("max_ready")
        mrow_turned, mrow_ready = sem("mrow_turned"), sem("mrow_ready")
        s_ready, p_exp, p_ready, pv_done = sem("s_ready"), sem("p_exp"), sem("p_ready"), sem("pv_done")
        rden_ready, prompt_out = sem("rden_ready"), sem("prompt_out")
        ss_scores, ss_max, ss_exp, ss_probs = sem("sample_scores"), sem("sample_max"), sem("sample_exp"), sem("sample_probs")
        ss_turned, ss_pt, ss_pv, attn_out = sem("sample_turned"), sem("sample_pt"), sem("sample_pv"), sem("attn_out")
        mid_ready = sem("mid_ready")
        mix_hi, mix_ready = sem("mix_hi"), sem("mix_ready")
        silu_ready, ff_ready = sem("silu_ready"), sem("ff_ready")
        y_zeroed = sem("y_zeroed")
        out_turned, out_staged = sem("out_turned"), sem("out_staged")
        out_stored = sem("out_stored")

        CONSTS = 16 * 26

        block = ctx.enter_context(nc.Block())

        @block.sync
        def _(sp):
            w_in = a["w_in"].rearrange("l (k p) c -> l p k c", p=P)
            w_fi = a["w_ffn_in"].rearrange("l (k p) c -> l p k c", p=P)
            w_o = a["w_out"].rearrange("l (k p) c -> l p k c", p=P)
            w_uq = a["w_uq"].rearrange("l (k p) (h c) -> l p k h c", p=P, h=HEADS)
            w_ukv = a["w_ukv"].rearrange("l (k p) c -> l p k c", p=P)

            def slab(l, slot, use, source):
                sp.wait_ge(raw_free[slot], l * SLOT_USES[slot] + use + 1)
                dst = RAW[:, slot * SLAB:(slot + 1) * SLAB]
                if len(source.shape) == 4:
                    dst, source = dst.rearrange("p (k c) -> p k c", k=KT), source.rearrange("l p k c -> (l p) k c")
                sp.dma_start(dst, source).then_inc(raw_landed[slot], 16)

            with sp.Fori(0, LAYERS) as l:
                one = bass.ds(l, 1)
                sp.wait_ge(raw_free[0], l * SLOT_USES[0] + 1)
                g = RAW[:, 0:SLAB].rearrange("p (k c) -> p k c", k=KT)
                for dst, src, n in ((0, COL_G, 8), (32, COL_G + 8, 8), (64, COL_KR, 32), (96, COL_KR + 16, 16), (112, COL_KR, 16)):
                    sp.dma_start(g[:, :, dst:dst + n], w_in[one, :, :, src:src + n].rearrange("l p k c -> (l p) k c")).then_inc(gate_raw_landed, 16)
                with sp.Fori(0, PAIRS) as p:
                    for i, col in enumerate((COL_Q, COL_K, COL_V, COL_O)):
                        slab(l, i % 2, SLOT_PAIRS[i % 2] + 2 * p + i // 2, w_in[one, :, :, bass.ds(p * P + col, P)])
                for i in range(4):
                    slab(l, i % 2, SLOT_LATENT[i % 2] + i // 2, w_in[one, :, :, COL_CQ + i * P:COL_CQ + (i + 1) * P])
                with sp.Fori(0, PAIRS) as p:
                    sp.wait_ge(raw_free[0], l * SLOT_USES[0] + SLOT_HEADS[0] + p + 1)
                    hs = RAW[:, 0:SLAB].rearrange("p (k c) -> p k c", k=2)
                    for h in range(2):
                        b = h * 256
                        for dst, src, n in ((0, 0, 96), (96, 80, 16), (112, 64, 16)):
                            sp.dma_start(hs[:, :, b + dst:b + dst + n],
                                         w_uq[one, :, :, bass.ds(2 * p + h, 1), src:src + n].rearrange("l p k h c -> (l p) k (h c)"))\
                              .then_inc(head_raw_landed, 16)
                        sp.dma_start(hs[:, :, b + 128:b + 256],
                                     w_ukv[one, :, :, bass.ds(p * 256 + h * 128, 128)].rearrange("l p k c -> (l p) k c")).then_inc(head_raw_landed, 16)
                with sp.Fori(0, KT // 2) as m:
                    for i in range(2):
                        slab(l, i, SLOT_OUT[i] + m, w_o[one, :, :, bass.ds(m * 256 + i * P, P)])

                def ffn_in(slot, use, tile, up):
                    slab(l, slot, use, w_fi[one, :, :, bass.ds(tile * P + up * DFF, P)])

                def ffn_out(slot, use, tile):
                    slab(l, slot, use, a["w_ffn_out"][one, bass.ds(tile * P, P), :].rearrange("l p c -> (l p) c"))
                u0, u1 = SLOT_FFN
                ffn_in(0, u0, 0, 0)
                with sp.Fori(0, FG - 1) as g_:
                    ffn_in(1, u1 + 3 * g_, 2 * g_, 1)
                    ffn_in(0, u0 + 1 + 3 * g_, 2 * g_ + 1, 0)
                    ffn_in(1, u1 + 1 + 3 * g_, 2 * g_ + 1, 1)
                    ffn_in(0, u0 + 2 + 3 * g_, 2 * g_ + 2, 0)
                    ffn_out(1, u1 + 2 + 3 * g_, 2 * g_)
                    ffn_out(0, u0 + 3 + 3 * g_, 2 * g_ + 1)
                n = 3 * (FG - 1)
                ffn_in(1, u1 + n, FT - 2, 1)
                ffn_in(0, u0 + 1 + n, FT - 1, 0)
                ffn_in(1, u1 + 1 + n, FT - 1, 1)
                ffn_out(0, u0 + 2 + n, FT - 2)
                ffn_out(1, u1 + 2 + n, FT - 1)

        @block.gpsimd
        def _(pool):
            for s in range(2):
                pool.memset(RAW[:, s * SLAB:(s + 1) * SLAB], 0.0).then_inc(raw_free[s], 1)

            pool.wait_ge(const_loaded, CONSTS)

            def split(l, slot, use, landed, count):
                pool.wait_ge(landed, count)
                pool.wait_ge(slab_free[slot], l * SLOT_USES[slot] + use + 1)
                raw, hi, lo = (t[:, slot * SLAB:(slot + 1) * SLAB] for t in (RAW, SH, SL))
                pool.tensor_tensor(hi, raw, ONES[:, 0:1].broadcast_to([P, SLAB]), ALU.mult)
                pool.drain()
                pool.tensor_tensor(lo, raw, hi, ALU.subtract).then_inc(slab_ready[slot], 1)
                pool.drain().then_inc(raw_free[slot], 1)

            def plain_split(l, slot, use, skipped=0):
                per_layer = PLAIN_0 if slot == 0 else SLOT_USES[1]
                split(l, slot, use, raw_landed[slot], (l * per_layer + use - skipped + 1) * 16)

            with pool.Fori(0, LAYERS) as l:
                split(l, 0, 0, gate_raw_landed, (l + 1) * 16 * 5)
                with pool.Fori(0, PAIRS) as p:
                    for i in range(4):
                        plain_split(l, i % 2, SLOT_PAIRS[i % 2] + 2 * p + i // 2, 1 - i % 2)
                for i in range(4):
                    plain_split(l, i % 2, SLOT_LATENT[i % 2] + i // 2, 1 - i % 2)
                with pool.Fori(0, PAIRS) as p:
                    split(l, 0, SLOT_HEADS[0] + p, head_raw_landed, (l * PAIRS + p + 1) * 16 * 8)
                with pool.Fori(0, KT // 2) as m:
                    for i in range(2):
                        plain_split(l, i, SLOT_OUT[i] + m, 5 if i == 0 else 0)
                u0, u1 = SLOT_FFN
                plain_split(l, 0, u0, 5)
                with pool.Fori(0, 11 - 1) as g:
                    for i in range(3):
                        plain_split(l, 1, u1 + 3 * g + i)
                        plain_split(l, 0, u0 + 1 + 3 * g + i, 5)
                for i, slot in enumerate((1, 0, 1, 0, 1)):
                    use = (u0 + 1 if slot == 0 else u1) + 3 * (FG - 1) + i // 2
                    plain_split(l, slot, use, 5 if slot == 0 else 0)

        @block.tensor
        def _(pe):
            def three(out, wh, wl, xh, xl, first, last):
                pe.matmul(out, wh, xh, start=first, stop=False)
                pe.matmul(out, wl, xh, start=False, stop=False)
                return pe.matmul(out, wh, xl, start=False, stop=last)

            def wait_slab(l, slot, use):
                pe.wait_ge(slab_ready[slot], l * SLOT_USES[slot] + use + 1)

            def wait_set(l, s, use):
                pe.wait_ge(emptied[s], l * SET_USES[s] + use + 1)

            def product(l, slot, slot_use, s, set_use):
                wait_slab(l, slot, slot_use)
                wait_set(l, s, set_use)
                for n in range(NG):
                    for k in range(KT):
                        w = slice(slot * SLAB + k * P, slot * SLAB + (k + 1) * P)
                        x = slice(k * T + n * TG, k * T + (n + 1) * TG)
                        mm = three(bank(3 * s + n, TG), SH[:, w], SL[:, w], HH[:, x], HL[:, x], k == 0, k == KT - 1)
                return mm

            def mean_square(l, i, summed, count):
                pe.wait_ge(summed, count)
                for n in range(NG):
                    mm = pe.matmul(bank(n, TG), ONES[:, :], SS[:, n * TG:(n + 1) * TG], start=True, stop=True)
                mm.then_inc(ms_ready, 1)

            pe.wait_ge(const_loaded, CONSTS)
            for c in range(CH):
                w = P if c < CH - 1 else DEC
                pe.wait_ge(x_loaded, 32)
                if c >= 4:
                    pe.wait_ge(in_taken, c - 3)
                for k in range(KT):
                    src = Y[:, c * D + k * P:c * D + (k + 1) * P] if c < CH - 1 else W2[0:DEC, k * P:(k + 1) * P]
                    mm = pe.transpose(bank(2 * (c % 4), w, off=k * P), src, IDN[0:w, 0:w])
                mm.then_inc(in_turned, 1)
            pe.wait_ge(in_taken, CH)

            with pe.Fori(0, LAYERS) as l:
                mean_square(l, 0, sq_added, l * SUMS + KT - 1)
                pe.wait_ge(h_ready, l * 2 * KT + KT)
                mm = product(l, 0, 0, 0, 0)
                mm.then_inc(tile_done, 1)
                pe.drain().then_inc(slab_free[0], 1)
                pe.wait_ge(gate_exps, l * 4 + 4)
                for c in range(CH):
                    mm = pe.transpose(PS[:, c * P:(c + 1) * P], X[:, G4 + c * P:G4 + (c + 1) * P], IDN[:, :])
                for j in range(PAIRS):
                    mm = pe.matmul(bank(3, CH, off=j * CH), SEL[:, j * P:(j + 1) * P], SMALL[0:8, 40:40 + CH], start=True, stop=True)
                mm.then_inc(gate_turned, 1)
                with pe.Fori(0, PAIRS) as p:
                    u = l * PAIRS + p
                    pe.wait_ge(gates_ready, l + 1)
                    pe.wait_ge(mout_done, u * 3 + 1)
                    for i in range(4):
                        s = (1 + i) % 2
                        product(l, i % 2, SLOT_PAIRS[i % 2] + 2 * p + i // 2, s,
                                SET_PAIRS[s] + 2 * p + i // 2).then_inc(tile_done, 1)
                        pe.drain().then_inc(slab_free[i % 2], 1)
                    wait_set(l, 1, SET_PAIRS[1] + 2 * p + 2)
                    pe.wait_ge(mixer_cleared, l + 1)
                    for c in range(CH):
                        mm = pe.transpose(PS[:, 3 * BANK + c * P:3 * BANK + (c + 1) * P], X[:, 2 * TP + c * P:2 * TP + (c + 1) * P], IDN[:, :])
                    mm.then_inc(kv_turned, 1)
                    wait_set(l, 0, SET_PAIRS[0] + 2 * p + 2)
                    for c in range(CH):
                        mm = pe.transpose(PS[:, c * P:(c + 1) * P], X[:, TP + c * P:TP + (c + 1) * P], IDN[:, :])
                    mm.then_inc(kv_turned, 1)
                    pe.wait_ge(vx_ready, u + 1)
                    pe.wait_ge(kw_ready, u + 1)
                    for c in range(CH):
                        mm = pe.matmul(bank(c // CG, 2 * HB, off=c % CG * 2 * HB), KW[:, c * P:(c + 1) * P],
                                       VX[:, c * 2 * HB:(c + 1) * 2 * HB], start=True, stop=True)
                    mm.then_inc(upd_ready, 1)
                    pe.wait_ge(states_ready, u + 1)
                    for g in range(3):
                        n = u * 3 + g
                        pe.wait_ge(um_ready, n + 1)
                        for h in range(2):
                            mm = pe.matmul(bank(3 + h, 3 * P), ONES[0:8, :], UM[0:8, h * 384:(h + 1) * 384], start=True, stop=True)
                        mm.then_inc(u_ready, 1)
                        for h in range(2):
                            r = slice(64 * h, 64 * h + 64)
                            for c in range(CG):
                                t = slice((g * CG + c) * P, (g * CG + c + 1) * P)
                                mm = pe.matmul(bank(5 + h, P, off=c * P), X[r, TP + t.start:TP + t.stop], X[r, t], start=True, stop=True)
                        mm.then_inc(st_ready, 1)
                        for c in range(CG):
                            t = (g * CG + c) * P
                            state = cs(g * CG + c) if g * CG + c < CH - 1 else cs(10)
                            mm = pe.matmul(bank(0, 2 * HB, off=c * 2 * HB), X[:, t:t + P], state, start=True, stop=True)
                        pe.wait_ge(w_ready, n + 1)
                        for h in range(2):
                            for c in range(CG):
                                j = (g * CG + c) * 2 * HB + h * HB
                                mm = pe.matmul(bank(7, HB, off=(2 * c + h) * HB), WT[:, (3 * h + c) * P:(3 * h + c + 1) * P],
                                               VX[:, j:j + HB], start=True, stop=True)
                        mm.then_inc(num_ready, 1)
                        pe.wait_ge(hn_ready, n + 1)
                        for c in range(CG):
                            mm = pe.transpose(bank(1, P, off=c * P), HBUF[:, c * P:(c + 1) * P], IDN[:, :])
                        mm.then_inc(ht_ready, 1)

                pe.wait_ge(mout_done, l * PAIRS * 3 + PAIRS * 3 + 1)
                for i in range(4):
                    s = (1 + i) % 2
                    product(l, i % 2, SLOT_LATENT[i % 2] + i // 2, s, SET_LATENT[s] + i // 2).then_inc(tile_done, 1)
                    pe.drain().then_inc(slab_free[i % 2], 1)
                mean_square(l, 1, csq_added, l * 2 + 1)
                mean_square(l, 2, csq_added, l * 2 + 2)
                pe.wait_ge(cache_loaded, (l + 1) * 32)
                for kt in range(2):
                    for t in range(8):
                        mm = pe.transpose(PS[:, 3 * BANK + (kt * 8 + t) * P:3 * BANK + (kt * 8 + t + 1) * P],
                                          Y[:, CACHE + t * 256 + kt * P:CACHE + t * 256 + (kt + 1) * P], IDN[:, :])
                mm.then_inc(cache_turned, 1)
                pe.wait_ge(rs_ready, l * NORMS + 3)
                for t in range(8):
                    mm = pe.transpose(PS[0:ROPE, t * P:(t + 1) * P], Y[:, CACHE + 2048 + t * ROPE:CACHE + 2048 + (t + 1) * ROPE], IDN[:, :])
                mm.then_inc(kr_turned, 1)
                pe.wait_ge(kr_full, l + 1)
                pe.wait_ge(lat_scaled, l * 4 + 4)
                pe.wait_ge(cache_lo, l + 1)
                for c in range(CH):
                    w = P if c < CH - 1 else DEC
                    n = l * CH + c
                    if c >= 2:
                        pe.wait_ge(nat_staged, n - 1)
                    for j in range(2):
                        pe.transpose(bank(c % 2, P, (0, w), j * P), X[:, (2 + j) * T + c * P:(2 + j) * T + c * P + w], IDN[:, :])
                    pe.transpose(bank(c % 2, ROPE, (0, w), 2 * P), X[64:96, KRF + c * P:KRF + c * P + w], IDN[64:96, 64:96])\
                        .then_inc(nat_turned, 1)
                with pe.Fori(0, PAIRS) as p:
                    pe.wait_ge(keys_ready, l + 1)
                    pe.wait_ge(lat_ready, l * 4 + 4)
                    pe.wait_ge(nat_staged, l * CH + CH)
                    wait_slab(l, 0, SLOT_HEADS[0] + p)
                    for h in range(2):
                        hd = (l * PAIRS + p) * 2 + h
                        pe.wait_ge(attn_out, hd + 1)
                        for n in range(NG):
                            for k in range(2):
                                w = slice(k * 512 + h * 256, k * 512 + h * 256 + P)
                                x = slice(CQ + k * T + n * TG, CQ + k * T + (n + 1) * TG)
                                mm = three(bank(n, TG), SH[:, w], SL[:, w], HH[:, x], HL[:, x], k == 0, k == 1)
                        mm.then_inc(q_proj, 1)
                        for n in range(5):
                            for k in range(2):
                                w = slice(k * 512 + h * 256 + P, k * 512 + h * 256 + 2 * P)
                                x = slice(CKV + k * KEYS + n * 416, CKV + k * KEYS + (n + 1) * 416)
                                mm = three(bank(3 + n, 416), SH[:, w], SL[:, w], HH[:, x], HL[:, x], k == 0, k == 1)
                        mm.then_inc(kv_proj, 1)
                        if h == 1:
                            pe.drain().then_inc(slab_free[0], 1)
                        pe.wait_ge(vt_ready, hd + 1)
                        pe.wait_ge(qf_ready, hd + 1)
                        for t in range(17):
                            k0, w = (t * P, P) if t < 8 else (T + (t - 8) * P, P) if t < 16 else (SEQ, DEC)
                            out, src = PS[0:w, t * HD:(t + 1) * HD], X[64:128, VTF + k0:VTF + k0 + w]
                            if t == 0:
                                pe.matmul(out, src, IDN[64:128, 64:128], start=True, stop=True)
                            else:
                                mm = pe.transpose(out, src, IDN[64:128, 64:128])
                        mm.then_inc(v_turned, 1)
                        pe.wait_ge(qk_ready, hd * 2 + 2)
                        for i in range(8):
                            if i >= 2:
                                pe.wait_ge(smax_taken, hd * 8 + i - 1)
                            q = RH[0:96, QTO + i * P:QTO + (i + 1) * P]
                            end = (i + 1) * P
                            for k0 in range(0, end, BANK):
                                k1 = min(end, k0 + BANK)
                                mm = pe.matmul(bank(3 + 2 * (i % 2) + k0 // BANK, k1 - k0), q, HH[0:96, KTO + k0:KTO + k1], start=True, stop=True)
                            mm.then_inc(smax_ready, 1)
                        pe.wait_ge(v_ready, hd + 1)
                        pe.wait_ge(max_ready, hd + 1)
                        for i in range(8):
                            mm = pe.matmul(PS[0:1, i * P:(i + 1) * P], SMALL[:, i:i + 1], IDN[:, :], start=True, stop=True)
                        mm.then_inc(mrow_turned, 1)
                        pe.wait_ge(mrow_ready, hd + 1)

                        def scores(b):
                            kt, q0, q1 = BLOCKS[b]
                            if b >= 4:
                                pe.wait_ge(p_exp, hd * NB + b - 3)
                            k, q = slice(KTO + kt * P, KTO + (kt + 1) * P), slice(QTO + q0, QTO + q1)
                            three(bank(2 + b % 4, q1 - q0), HH[0:97, k], HL[0:97, k], RH[0:97, q], RL[0:97, q], True, True)\
                                .then_inc(s_ready, 1)

                        def weigh(b):
                            kt, q0, q1 = BLOCKS[b]
                            w = q1 - q0
                            out = PS[:, 6 * BANK + q0:6 * BANK + q1]
                            v, pr = slice(VO + kt * P, VO + (kt + 1) * P), slice(PO + b % 2 * BANK, PO + b % 2 * BANK + w)
                            pe.wait_ge(p_ready, hd * NB + b + 1)
                            first, last = kt == 0, kt == (3 if q0 < 512 else 7)
                            pe.matmul(out, RH[:, v], RH[:, pr], start=first, stop=False)
                            pe.matmul(out, RL[:, v], RH[:, pr], start=False, stop=False)
                            pe.matmul(out, RH[:, v], RL[:, pr], start=False, stop=last).then_inc(pv_done, 1)
                        for b in range(NB + 2):
                            if b < NB:
                                scores(b)
                            if b >= 2:
                                weigh(b - 2)
                        pe.wait_ge(p_exp, hd * NB + NB)
                        for n in range(NG):
                            k, q = slice(KTO + SEQ + n * TG, KTO + SEQ + (n + 1) * TG), slice(QTO + SEQ, QTO + T)
                            mm = three(bank(n, TG, (0, DEC)), RH[0:96, q], RL[0:96, q], HH[0:96, k], HL[0:96, k], True, True)
                        mm.then_inc(ss_scores, 1)
                        pe.wait_ge(ss_probs, hd + 1)
                        for t in range(8):
                            out, src = bank(3, DEC, off=t * DEC), SS[0:DEC, DEC + t * P:DEC + (t + 1) * P]
                            if t == 0:
                                pe.matmul(out, src, IDN[0:DEC, 0:DEC], start=True, stop=True)
                            else:
                                pe.transpose(out, src, IDN[0:DEC, 0:DEC])
                        pe.transpose(bank(3, DEC, (0, DEC), 8 * DEC), SS[0:DEC, 0:DEC], IDN[0:DEC, 0:DEC]).then_inc(ss_turned, 1)
                        pe.wait_ge(ss_pt, hd + 1)
                        for t in range(8):
                            pe.matmul(bank(4, DEC, (0, HD)), X[:, VS + t * HD:VS + (t + 1) * HD], X[:, PTS + t * DEC:PTS + (t + 1) * DEC],
                                      start=t == 0, stop=False)
                        pe.matmul(bank(4, DEC, (0, HD)), X[0:DEC, VS + 8 * HD:VS + 9 * HD], X[0:DEC, PTS + 8 * DEC:PTS + 9 * DEC],
                                  start=False, stop=True).then_inc(ss_pv, 1)

                with pe.Fori(0, KT // 2) as m:
                    pe.wait_ge(mix_ready, (l + 1) * KT)
                    for i in range(2):
                        product(l, i, SLOT_OUT[i] + m, i, SET_OUT[i] + m).then_inc(tile_done, 1)
                        pe.drain().then_inc(slab_free[i], 1)
                mean_square(l, 3, sq_added, l * SUMS + 2 * (KT - 1))
                mean_square(l, 4, sq_added, l * SUMS + 3 * (KT - 1))
                pe.wait_ge(h_ready, (l + 1) * 2 * KT)

                def inner(slot, slot_use, s, set_use):
                    product(l, slot, slot_use, s, set_use).then_inc(tile_done, 1)
                    pe.drain().then_inc(slab_free[slot], 1)

                def outer(g, slots, s0, set_uses):
                    for slot, use in slots:
                        wait_slab(l, slot, use)
                    pe.wait_ge(ff_ready, (l * FG + g + 1) * 2)
                    for m in range(KT):
                        s = (s0 + m) % 2
                        wait_set(l, s, set_uses[s] + m // 2)
                        for n in range(NG):
                            for j in range(2):
                                slot = slots[j][0]
                                w = slice(slot * SLAB + m * P, slot * SLAB + (m + 1) * P)
                                x = slice(j * T + n * TG, j * T + (n + 1) * TG)
                                mm = three(bank(3 * s + n, TG), SH[:, w], SL[:, w], HHF(x), HLF(x), j == 0, j == 1)
                        mm.then_inc(tile_done, 1)
                    for slot, _ in slots:
                        pe.drain().then_inc(slab_free[slot], 1)

                def HHF(x):
                    return RH[:, x]

                def HLF(x):
                    return RL[:, x]

                u0, u1 = SLOT_FFN
                s0, s1 = SET_FFN
                inner(0, u0, 0, s0)
                with pe.Fori(0, FG - 1) as g:
                    inner(1, u1 + 3 * g, 1, s1 + 6 * g)
                    inner(0, u0 + 1 + 3 * g, 0, s0 + 1 + 6 * g)
                    inner(1, u1 + 1 + 3 * g, 1, s1 + 1 + 6 * g)
                    inner(0, u0 + 2 + 3 * g, 0, s0 + 2 + 6 * g)
                    outer(g, ((1, u1 + 2 + 3 * g), (0, u0 + 3 + 3 * g)), 1, (s0 + 3 + 6 * g, s1 + 2 + 6 * g))
                n3, n6 = 3 * (FG - 1), 6 * (FG - 1)
                inner(1, u1 + n3, 1, s1 + n6)
                inner(0, u0 + 1 + n3, 0, s0 + 1 + n6)
                inner(1, u1 + 1 + n3, 1, s1 + 1 + n6)
                outer(FG - 1, ((0, u0 + 2 + n3), (1, u1 + 2 + n3)), 0, (s0 + 2 + n6, s1 + 2 + n6))
                mean_square(l, 5, sq_added, l * SUMS + 4 * (KT - 1))

            pe.wait_ge(x_ready, LAYERS + 1)
            for c in range(CH):
                w = P if c < CH - 1 else DEC
                if c >= 4:
                    pe.wait_ge(out_staged, c - 3)
                for k in range(KT):
                    mm = pe.transpose(bank(2 * (c % 4), P, (0, w), k * P), X[:, k * T + c * P:k * T + c * P + w], IDN[:, :])
                mm.then_inc(out_turned, 1)

        @block.scalar
        def _(act):
            def squares(l, i, src):
                for k in range(KT):
                    if k >= 2:
                        act.wait_ge(sq_added, l * SUMS + i * (KT - 1) + max(k - 2, 1))
                    act.activation(W2[:, (k % 2) * T:(k % 2 + 1) * T], src(k), ACT.Square).then_inc(sq_ready, 1)

            def rstd(l, i, width):
                act.wait_ge(ms_ready, l * NORMS + i + 1)
                act.activation(by(RS[:, :], 3), pset(0), ACT.Ln, bias=CONST[:, 0:1], scale=1.0 / width)
                act.drain()
                act.activation(RS[:, :], RS[:, :], ACT.Exp, scale=-0.5).then_inc(rs_ready, 1)

            def hi_of_h(l, i):
                for k in range(KT):
                    act.wait_ge(scaled, l * 2 * KT + i * KT + k + 1)
                    act.activation(HH[:, k * T:(k + 1) * T], W2[:, (k % 2) * T:(k % 2 + 1) * T], ACT.Copy).then_inc(hi_ready, 1)

            act.dma_start(IDN[:, :], a["identity"]).then_inc(const_loaded, 16)
            act.dma_start(CM[:, :], a["causal"]).then_inc(const_loaded, 16)
            act.dma_start(BM[:, :], a["pair_mask"]).then_inc(const_loaded, 16)
            act.dma_start(SEL[:, :], a["pair_select"]).then_inc(const_loaded, 16)
            act.dma_start(CONST[:, :], a["constants"]).then_inc(const_loaded, 16)
            act.dma_start(Y[:, 0:8 * D].rearrange("p (c d) -> p c d", c=8),
                          a["x_prompt"][0, :, :].rearrange("(c p) d -> p c d", p=P)).then_inc(x_loaded, 16)
            act.dma_start(W2[0:DEC, 0:D], a["x_sample"][0, :, :]).then_inc(x_loaded, 16)
            with nc.allow_non_contiguous_dma("gains, once"):
                for i, name in enumerate(("g_pre_mix", "g_post_mix", "g_pre_ffn", "g_post_ffn")):
                    for j in range(LAYERS):
                        act.dma_start(GN[:, (j * 4 + i) * KT:(j * 4 + i + 1) * KT], a[name][j, :].rearrange("(k p) -> p k", p=P),
                                      allow_slow_non_contiguous=True).then_inc(const_loaded, 16)
                act.dma_start(by(GM[:, :], LAYERS), a["g_mlstm_head"].rearrange("l (k p) -> p l k", p=P),
                              allow_slow_non_contiguous=True).then_inc(const_loaded, 16)
                for j in range(LAYERS):
                    act.dma_start(GC[:, 4 * j:4 * j + 2], a["g_q_norm"][j, :].rearrange("(k p) -> p k", p=P),
                                  allow_slow_non_contiguous=True).then_inc(const_loaded, 16)
                    act.dma_start(GC[:, 4 * j + 2:4 * j + 4], a["g_kv_norm"][j, :].rearrange("(k p) -> p k", p=P),
                                  allow_slow_non_contiguous=True).then_inc(const_loaded, 16)
                for j in range(LAYERS):
                    for c in range(2):
                        act.dma_start(BG[:, 3 * j + c:3 * j + c + 1], a["b_gates"][j, c * HEADS:(c + 1) * HEADS].unsqueeze(1),
                                      allow_slow_non_contiguous=True).then_inc(const_loaded, 16)
                    act.dma_start(BG[:, 3 * j + 2:3 * j + 3], a["state_mlstm_m"][j, 0, :].unsqueeze(1),
                                  allow_slow_non_contiguous=True).then_inc(const_loaded, 16)
                act.dma_start(ONES[:, :], a["ones"]).then_inc(const_loaded, 16)
                act.dma_start(SMALL[:, :], a["zeros"]).then_inc(const_loaded, 16)
            act.wait_ge(const_loaded, CONSTS)

            with act.Fori(0, LAYERS) as l:
                one = bass.ds(l, 1)
                act.wait_ge(x_ready, l + 1)
                act.dma_start(x_spill, X[:, :]).then_inc(x_spilled, 16)
                squares(l, 0, xt)
                rstd(l, 0, D)
                hi_of_h(l, 0)
                act.wait_ge(f_ready, l + 1)
                act.activation(gt(3, 0, T), gt(2, 0, T), ACT.Exp)
                act.drain()
                act.activation(gt(3, 0, T), gt(3, 0, T), ACT.Ln, bias=CONST[0:8, 1:2]).then_inc(softplus_ready, 1)
                act.wait_ge(args_ready, l + 1)
                act.activation(SMALL[0:8, 40:40 + CH], SMALL[0:8, 30:30 + CH], ACT.Exp)
                act.activation(X[0:8, G4:G4 + TP], gt(1), ACT.Exp).then_inc(gate_exps, 1)
                act.activation(X[32:40, G4:G4 + TP], gt(4), ACT.Exp).then_inc(gate_exps, 1)
                act.activation(X[64:72, G4:G4 + TP], gt(2), ACT.Exp, scale=-1.0).then_inc(gate_exps, 1)
                act.activation(X[96:104, G4:G4 + TP], gt(0), ACT.Copy).then_inc(gate_exps, 1)
                with nc.allow_non_contiguous_dma("last m of each head"):
                    act.dma_start(o["m_prompt"][one, 0, :].rearrange("l h -> h l"), SMALL[0:8, 7:8], allow_slow_non_contiguous=True).then_inc(m_stored, 16)
                    act.dma_start(o["m_sample"][one, 0, :].rearrange("l h -> h l"), SMALL[0:8, 8:9], allow_slow_non_contiguous=True).then_inc(m_stored, 16)

                with act.Fori(0, PAIRS) as p:
                    u = l * PAIRS + p
                    act.wait_ge(mixer_cleared, l + 1)
                    act.wait_ge(mout_done, u * 3 + 1)
                    act.wait_ge(state_stored, u * 128 + 16)
                    for h in range(2):
                        r, j = (64 * h, 64 * h + 64), HB * h
                        act.dma_start(cs(10, r, (j, j + HD)), a["state_mlstm_C"][one, 0, bass.ds(2 * p + h, 1), :, :].rearrange("l h d e -> (l h d) e"))\
                           .then_inc(state_loaded, 16)
                        act.dma_start(cs(10, r, (j + HD, j + HB)), a["state_mlstm_n"][one, 0, bass.ds(2 * p + h, 1), :].rearrange("l h d -> (l h d)").unsqueeze(1))\
                           .then_inc(state_loaded, 16)
                    act.wait_ge(tile_done, l * TILES + TILE_PAIRS + 4 * p + 4)
                    act.activation(by(OM, 3), pset(0), ACT.Sigmoid).then_inc(emptied[0], 1)
                    act.wait_ge(kv_turned, u * 2 + 1)
                    act.activation(VX.rearrange("p (c h e) -> p c h e", c=CH, h=2)[:, :, :, 0:HD],
                                   PS[:, 3 * BANK:3 * BANK + TP].rearrange("p (c h e) -> p c h e", c=CH, h=2), ACT.Copy).then_inc(vx_ready, 1)
                    for g in range(3):
                        n = u * 3 + g
                        act.wait_ge(dm_ready, n + 1)
                        for h in range(2):
                            for c in range(CG):
                                q = PT[:, (3 * h + c) * P:(3 * h + c + 1) * P]
                                e = act.activation(q, q, ACT.Exp, bias=N4[:, bass.ds((g * CG + c) * 32 + 24 + h + 2 * p, 1)])
                        e.then_inc(pt_ready, 1)
                        act.wait_ge(ms_head, n + 1)
                        act.activation(SMALL[:, 48:54], SMALL[:, 48:54], ACT.Ln, bias=CONST[:, 0:1], scale=1.0 / HD)
                        act.drain()
                        act.activation(SMALL[:, 48:54], SMALL[:, 48:54], ACT.Exp, scale=-0.5).then_inc(rr_ready, 1)
                    for i, (cn, nn, c) in enumerate((("C_prompt", "n_prompt", 8), ("C_sample", "n_sample", 9))):
                        for h in range(2):
                            r, j = (64 * h, 64 * h + 64), HB * h
                            act.dma_start(o[cn][one, 0, bass.ds(2 * p + h, 1), :, :].rearrange("l h d e -> (l h d) e"), cs(c, r, (j, j + HD)))\
                               .then_inc(state_stored, 16)
                            act.dma_start(o[nn][one, 0, bass.ds(2 * p + h, 1), :].rearrange("l h d -> (l h d)").unsqueeze(1), cs(c, r, (j + HD, j + HB)))\
                               .then_inc(state_stored, 16)

                act.wait_ge(mout_done, (l + 1) * PAIRS * 3 + 1)
                act.dma_start(X[64:128, TRIG:TRIG + T], a["trig"]).then_inc(trig_loaded, 16)
                act.dma_start(Y[:, CACHE:CACHE + 2048].rearrange("p (t c) -> p t c", t=8),
                              a["cache_ckv"][one, 0, :, :].rearrange("l (t p) c -> p (l t) c", p=P)).then_inc(cache_loaded, 16)
                act.dma_start(Y[:, CACHE + 2048:CACHE + 2304].rearrange("p (t c) -> p t c", t=8),
                              a["cache_krope"][one, 0, :, :].rearrange("l (t p) c -> p (l t) c", p=P)).then_inc(cache_loaded, 16)
                for i in range(2):
                    for j in range(2):
                        s = (1 + j) % 2
                        act.wait_ge(emptied[s], l * SET_USES[s] + SET_LATENT[s] + i + 2)
                    if i == 1:
                        act.wait_ge(csq_added, l * 2 + 1)
                    for j in range(2):
                        act.activation(W2[:, j * T:(j + 1) * T], X[:, (2 * i + j) * T:(2 * i + j + 1) * T], ACT.Square).then_inc(csq_ready, 1)
                    if i == 1:
                        act.wait_ge(lat_scaled, l * 4 + 2)
                    rstd(l, 1 + i, RANK)
                    for j in range(2):
                        act.wait_ge(lat_scaled, l * 4 + 2 * i + j + 1)
                        dst = CQ + j * T if i == 0 else CKV + j * KEYS
                        act.activation(HH[:, dst:dst + T], X[:, (2 * i + j) * T:(2 * i + j + 1) * T], ACT.Copy).then_inc(lat_hi, 1)
                act.wait_ge(cache_turned, l + 1)
                act.activation(HH[:, CKV:CKV + 2 * KEYS].rearrange("p (k c) -> p k c", k=2)[:, :, T:KEYS],
                               by(PS[:, 3 * BANK:3 * BANK + 2048], 2), ACT.Copy).then_inc(cache_hi, 1)
                act.wait_ge(kr_full, l + 1)
                act.activation(HH[64:96, KTO:KTO + KEYS], X[64:96, KRF:KRF + KEYS], ACT.Copy).then_inc(krope_hi, 1)
                for c in range(CH):
                    n = l * CH + c
                    act.wait_ge(nat_staged, n + 1)
                    st = STAGE + c % 3 * 288
                    if c < CH - 1:
                        act.dma_start(o["new_ckv_prompt"][one, 0, c * P:(c + 1) * P, :].rearrange("l t c -> (l t) c"), Y[:, st:st + 256]).then_inc(nat_stored[c % 3], 16)
                        act.dma_start(o["new_krope_prompt"][one, 0, c * P:(c + 1) * P, :].rearrange("l t c -> (l t) c"), Y[:, st + 256:st + 288]).then_inc(nat_stored[c % 3], 16)
                    else:
                        act.dma_start(o["new_ckv_sample"][one, 0, :, :].rearrange("l t c -> (l t) c"), Y[0:DEC, st:st + 256]).then_inc(nat_stored[c % 3], 16)
                        act.dma_start(o["new_krope_sample"][one, 0, :, :].rearrange("l t c -> (l t) c"), Y[0:DEC, st + 256:st + 288]).then_inc(nat_stored[c % 3], 16)

                with act.Fori(0, PAIRS) as p:
                    for h in range(2):
                        hd = (l * PAIRS + p) * 2 + h
                        act.wait_ge(q_proj, hd + 1)
                        act.activation(by(X[0:64, QF:QF + T], 3), pset(0, (0, 64)), ACT.Copy).then_inc(qnope_ready, 1)
                        kvp = PS[:, 3 * BANK:8 * BANK].rearrange("p (n c) -> p n c", n=5)[:, :, 0:416]
                        act.wait_ge(kv_proj, hd + 1)
                        act.activation(by(X[64:128, VTF:VTF + KEYS], 5), kvp[64:128], ACT.Copy).then_inc(vt_ready, 1)
                        act.activation(by(HH[0:64, KTO:KTO + KEYS], 5), kvp[0:64], ACT.Copy).then_inc(khi_ready, 1)
                        act.wait_ge(qf_ready, hd + 1)
                        act.activation(RH[0:96, QTO:QTO + T], X[0:96, QF:QF + T], ACT.Copy).then_inc(qhi_ready, 1)
                        act.wait_ge(v_turned, hd + 1)
                        act.activation(RH[:, VO:VO + SEQ].rearrange("p (t c) -> p t c", t=8)[:, :, 0:HD], by(PS[:, 0:512], 8), ACT.Copy).then_inc(vhi_ready, 1)
                        act.wait_ge(mrow_turned, hd + 1)
                        act.activation(RH[96:97, QTO:QTO + SEQ], PS[0:1, 0:SEQ], ACT.Copy, scale=-1.0).then_inc(mrow_ready, 1)
                        for b, (kt, q0, q1) in enumerate(BLOCKS):
                            w = q1 - q0
                            act.wait_ge(s_ready, hd * NB + b + 1)
                            if b >= 2:
                                act.wait_ge(p_ready, hd * NB + b - 1)
                            act.activation(X[:, PF + b % 2 * BANK:PF + b % 2 * BANK + w], bank(2 + b % 4, w), ACT.Exp, scale=SCALE).then_inc(p_exp, 1)
                        act.wait_ge(pv_done, hd * NB + NB)
                        act.activation(W2[0:64, 0:SEQ], PS[64:128, 6 * BANK:8 * BANK], ACT.Ln)
                        act.drain()
                        act.activation(W2[0:64, 0:SEQ], W2[0:64, 0:SEQ], ACT.Exp, scale=-1.0).then_inc(rden_ready, 1)
                        act.wait_ge(ss_max, hd + 1)
                        act.activation(by(SS[0:DEC, :], 3), pset(0, (0, DEC)), ACT.Exp, bias=SMALL[0:DEC, 21:22], scale=SCALE,
                                       accum_out=SMALL[0:DEC, 22:23]).then_inc(ss_exp, 1)

                act.wait_ge(attn_out, (l + 1) * HEADS + 1)
                act.dma_start(X[:, :], x_spill).then_inc(x_back, 16)
                for k in range(KT):
                    act.activation(HH[:, k * T:(k + 1) * T], yt(k), ACT.Copy).then_inc(mix_hi, 1)
                for s in range(2):
                    act.wait_ge(emptied[s], l * SET_USES[s] + SET_FFN[s] + 1)
                squares(l, 1, yt)
                rstd(l, 3, D)
                act.wait_ge(x_ready, l + 1)
                for k in range(KT):
                    pass
                act.wait_ge(mid_ready, l + 1)
                squares(l, 2, xt)
                rstd(l, 4, D)
                hi_of_h(l, 1)

                def silu(g, j, tile, set_use):
                    act.wait_ge(tile_done, l * TILES + TILE_FFN + tile + 1)
                    if j == 0:
                        act.wait_ge(ff_ready, (l * FG + g) * 2 + 1 - 1) if False else None
                    act.activation(by(W2[:, j * T:(j + 1) * T], 3), pset(0), ACT.Silu).then_inc(silu_ready, 1)

                act.wait_ge(h_ready, (l + 1) * 2 * KT)
                act.wait_ge(tile_done, l * TILES + TILE_FFN + 1)
                act.activation(by(W2[:, 0:T], 3), pset(0), ACT.Silu).then_inc(emptied[0], 1)
                with act.Fori(0, FG - 1) as g:
                    base = l * TILES + TILE_FFN + 12 * g
                    act.wait_ge(tile_done, base + 3)
                    act.wait_ge(ff_ready, (l * FG + g) * 2 + 1)
                    act.activation(by(W2[:, T:2 * T], 3), pset(0), ACT.Silu).then_inc(emptied[0], 1)
                    act.wait_ge(tile_done, base + 5)
                    act.activation(by(W2[:, 0:T], 3), pset(0), ACT.Silu).then_inc(emptied[0], 1)
                act.wait_ge(tile_done, l * TILES + TILE_FFN + 12 * (FG - 1) + 3)
                act.wait_ge(ff_ready, (l * FG + FG - 1) * 2 + 1)
                act.activation(by(W2[:, T:2 * T], 3), pset(0), ACT.Silu).then_inc(emptied[0], 1)
                for s in range(2):
                    act.wait_ge(emptied[s], (l + 1) * SET_USES[s] + 1)
                squares(l, 3, yt)
                rstd(l, 5, D)

            for c in range(CH):
                act.wait_ge(out_staged, c + 1)
                if c < CH - 1:
                    act.dma_start(o["y_prompt"][0, c * P:(c + 1) * P, :], Y[:, c * D:(c + 1) * D]).then_inc(out_stored, 16)
                else:
                    act.dma_start(o["y_sample"][0, :, :], W2[0:DEC, 0:D]).then_inc(out_stored, 16)
            act.wait_ge(out_stored, 16 * CH)
            act.wait_ge(m_stored, 32 * LAYERS)
            act.wait_ge(state_stored, 16 + 128 * PAIRS * LAYERS)
            for s in range(3):
                act.wait_ge(nat_stored[s], 32 * 3 * LAYERS)

        @block.vector
        def _(dve):
            def add_squares(l, i):
                for k in range(1, KT):
                    if k > 1:
                        dve.drain()
                    dve.wait_ge(sq_ready, (l * 4 + i) * KT + k + 1)
                    dve.tensor_tensor(SS[:, :], W2[:, 0:T] if k == 1 else SS[:, :], W2[:, (k % 2) * T:(k % 2 + 1) * T], ALU.add)\
                       .then_inc(sq_added, 1)

            def normed(l, i, norm):
                dve.wait_ge(rs_ready, l * NORMS + norm + 1)
                gain = 0 if i == 0 else 2

                def lo(k):
                    dve.wait_ge(hi_ready, l * 2 * KT + i * KT + k + 1)
                    dve.tensor_tensor(HL[:, k * T:(k + 1) * T], W2[:, (k % 2) * T:(k % 2 + 1) * T], HH[:, k * T:(k + 1) * T], ALU.subtract)\
                       .then_inc(h_ready, 1)
                for k in range(KT):
                    if k >= 2:
                        dve.drain()
                    dve.scalar_tensor_tensor(out=W2[:, (k % 2) * T:(k % 2 + 1) * T], in0=xt(k),
                                             scalar=GN[:, bass.ds((l * 4 + gain) * KT + k, 1)], in1=RS[:, :], op0=ALU.mult, op1=ALU.mult)\
                       .then_inc(scaled, 1)
                    if k >= 1:
                        dve.drain()
                        lo(k - 1)
                dve.drain()
                lo(KT - 1)

            def residual(l, norm, gain, signal):
                dve.wait_ge(rs_ready, l * NORMS + norm + 1)
                for k in range(KT):
                    dve.scalar_tensor_tensor(out=yt(k), in0=yt(k), scalar=GN[:, bass.ds((l * 4 + gain) * KT + k, 1)], in1=RS[:, :],
                                             op0=ALU.mult, op1=ALU.mult)
                    dve.drain()
                    x = dve.tensor_tensor(xt(k), xt(k), yt(k), ALU.add)
                x.then_inc(signal, 1)

            for s in range(2):
                dve.memset(SH[:, s * SLAB:(s + 1) * SLAB].bitcast(F32), 0.0).then_inc(slab_free[s], 1)
                dve.memset(RS[:, 32 + 8 * s:40 + 8 * s], 0.0).then_inc(emptied[s], 1)
            dve.memset(RS[:, 0:8], 0.0).then_inc(mout_done, 1)
            dve.memset(RS[:, 8:16], 0.0).then_inc(attn_out, 1)
            dve.memset(RS[:, 16:24], 0.0).then_inc(state_stored, 16)
            dve.wait_ge(const_loaded, CONSTS)
            for c in range(CH):
                w = P if c < CH - 1 else DEC
                dve.wait_ge(in_turned, c + 1)
                src = PS[:, 2 * (c % 4) * BANK:2 * (c % 4 + 1) * BANK].rearrange("p (k c) -> p k c", k=KT)[:, :, 0:w]
                dve.tensor_copy(X[:, :].rearrange("p (k c) -> p k c", k=KT)[:, :, c * P:c * P + w], src).then_inc(in_taken, 1)
            dve.drain()
            dve.memset(RS[:, 24:32], 0.0).then_inc(x_ready, 1)

            with dve.Fori(0, LAYERS) as l:
                add_squares(l, 0)
                normed(l, 0, 0)

                bias = lambda i: BG[:, bass.ds(l * 3 + i, 1)]
                g3 = lambda i: by(gt(i, 0, T), 3)
                dve.wait_ge(x_spilled, (l + 1) * 16)
                dve.wait_ge(tile_done, l * TILES + 1)
                dve.tensor_copy(by(Y[64:128, KRRAW:KRRAW + T], 3), pset(0, (64, 128)))
                dve.tensor_scalar(g3(0), pset(0, (0, 8)), bias(0), None, ALU.add)
                dve.memset(gt(0, T, TP), NEG)
                dve.tensor_copy(g3(1), pset(0, (32, 40))).then_inc(emptied[0], 1)
                dve.drain()
                dve.tensor_scalar(gt(1, 0, T), gt(1, 0, T), bias(1), None, ALU.add)
                dve.drain()
                dve.scalar_tensor_tensor(out=gt(2, 0, T), in0=gt(1, 0, T), scalar=-1.0, in1=gt(1, 0, T), op0=ALU.mult, op1=ALU.min).then_inc(f_ready, 1)
                dve.memset(gt(4), 1.0)
                dve.memset(X[:, G4:G4 + TP], 0.0)
                dve.drain()
                dve.memset(gt(4).rearrange("p (c t) -> p c t", c=CH)[:, :, 0:1], 0.0)
                dve.wait_ge(softplus_ready, l + 1)
                dve.scalar_tensor_tensor(out=gt(1, 0, T), in0=gt(1, 0, T), scalar=0.0, in1=gt(3, 0, T), op0=ALU.min, op1=ALU.subtract)
                dve.memset(gt(1, T, TP), 0.0)
                dve.drain()
                dve.tensor_tensor_scan(gt(2, 0, SEQ), gt(1, 0, SEQ), gt(0, 0, SEQ), 0.0, ALU.add, ALU.max)
                dve.tensor_tensor_scan(gt(2, SEQ, TP), gt(1, SEQ, TP), gt(0, SEQ, TP), bias(2), ALU.add, ALU.max)
                dve.tensor_tensor_scan(gt(3), gt(4), gt(1), 0.0, ALU.mult, ALU.add)
                dve.drain()
                dve.tensor_tensor(UROW[:, :], gt(3), gt(2), ALU.subtract)
                dve.tensor_copy(SMALL[0:8, 0:8], gt(2, 0, SEQ).rearrange("p (c t) -> p c t", c=8)[:, :, 127:128].rearrange("p c t -> p (c t)"))
                dve.tensor_copy(SMALL[0:8, 8:9], gt(2, T - 1, T))
                dve.tensor_copy(SMALL[0:8, 10:18], gt(3, 0, SEQ).rearrange("p (c t) -> p c t", c=8)[:, :, 127:128].rearrange("p c t -> p (c t)"))
                dve.tensor_copy(SMALL[0:8, 18:19], gt(3, T - 1, T))
                dve.memset(SMALL[0:8, 20:21], 0.0)
                dve.tensor_copy(SMALL[0:8, 28:29], bias(2))
                dve.tensor_tensor(gt(0), gt(0), gt(3), ALU.subtract)
                dve.drain()
                dve.tensor_copy(SMALL[0:8, 21:28], SMALL[0:8, 0:7])
                dve.tensor_tensor(SMALL[0:8, 10:19], SMALL[0:8, 10:19], SMALL[0:8, 0:9], ALU.subtract)
                dve.drain()
                dve.tensor_tensor(SMALL[0:8, 30:39], SMALL[0:8, 10:19], SMALL[0:8, 20:29], ALU.add)
                c9 = lambda ap: ap.rearrange("p (c t) -> p c t", c=CH)
                over = lambda ap: ap.unsqueeze(2).broadcast_to([8, CH, P])
                dve.tensor_tensor(c9(gt(1)), c9(UROW[:, :]), over(SMALL[0:8, 20:29]), ALU.add)
                dve.tensor_tensor(c9(gt(4)), c9(gt(0)), over(SMALL[0:8, 10:19]), ALU.add)
                dve.drain()
                dve.memset(SMALL[0:8, 60:61], 0.0).then_inc(args_ready, 1)
                dve.wait_ge(gate_turned, l + 1)
                dve.tensor_copy(N4[:, :].rearrange("p (c q h) -> p c q h", c=CH, q=4),
                                PS[:, 0:TP].rearrange("p (c q h) -> p c q h", c=CH, q=4)[:, :, :, 0:8])
                dve.tensor_copy(DEC_ALL[:, :], bank(3, PAIRS * CH))
                dve.drain()
                dve.memset(SMALL[0:8, 60:61], 0.0).then_inc(gates_ready, 1)
                for i in range(3):
                    dve.memset(X[:, i * TP + T:(i + 1) * TP], 0.0)
                dve.memset(VX, 1.0)
                dve.wait_ge(gate_turned, l + 1)
                dve.memset(CS, 0.0)
                dve.drain()
                dve.memset(SMALL[0:8, 60:61], 0.0).then_inc(mixer_cleared, 1)

                with dve.Fori(0, PAIRS) as p:
                    u = l * PAIRS + p
                    tile = l * TILES + TILE_PAIRS + 4 * p
                    dve.wait_ge(tile_done, tile + 1)
                    dve.tensor_copy(by(X[:, 0:T], 3), pset(1)).then_inc(emptied[1], 1)
                    dve.wait_ge(tile_done, tile + 2)
                    dve.tensor_scalar(by(X[:, TP:TP + T], 3), pset(0), HD ** -0.5, None, ALU.mult).then_inc(emptied[0], 1)
                    dve.wait_ge(tile_done, tile + 3)
                    dve.tensor_copy(by(X[:, 2 * TP:2 * TP + T], 3), pset(1)).then_inc(emptied[1], 1)

                    def per_token(q, c0, c1, inner):
                        cols = N4[:, :].rearrange("p (c j) -> p c j", c=CH)[:, c0:c1, bass.ds(2 * p + 8 * q, 2)]
                        return cols.unsqueeze(3).broadcast_to([P, c1 - c0, 2, inner])
                    dve.wait_ge(kv_turned, u * 2 + 2)
                    dve.tensor_tensor(KW.rearrange("p (c h e) -> p c h e", c=CH, h=2),
                                      PS[:, 0:TP].rearrange("p (c h e) -> p c h e", c=CH, h=2), per_token(1, 0, CH, HD), ALU.mult).then_inc(kw_ready, 1)
                    dve.wait_ge(upd_ready, u + 1)
                    dve.wait_ge(state_loaded, (u + 1) * 64)
                    dve.wait_ge(state_stored, u * 128 + 16)
                    dve.tensor_tensor(X[:, C0 + 2 * HB:C0 + 10 * 2 * HB].rearrange("p (g c e) -> p g c e", g=3, c=3),
                                      PS[:, 0:3 * BANK].rearrange("p (g r) -> p g r", g=3)[:, :, 0:6 * HB].rearrange("p g (c e) -> p g c e", c=3),
                                      BM[:, :].unsqueeze(1).unsqueeze(1).broadcast_to([P, 3, 3, 2 * HB]), ALU.mult)
                    for c in range(1, CH):
                        src, dst = (c, c + 1) if c < CH - 1 else (10, 9)
                        dve.drain()
                        s = dve.scalar_tensor_tensor(out=cs(dst), in0=cs(src), scalar=DEC_ALL[:, bass.ds(p * CH + c, 1)], in1=cs(dst),
                                                     op0=ALU.mult, op1=ALU.add)
                    s.then_inc(states_ready, 1)
                    for g in range(3):
                        n = u * 3 + g
                        for h in range(2):
                            m = dve.tensor_scalar(UM[0:8, h * 384:(h + 1) * 384], UROW[:, g * 384:(g + 1) * 384],
                                                  IDN[0:8, bass.ds(2 * p + h, 1)], None, ALU.mult)
                        m.then_inc(um_ready, 1)
                        dve.wait_ge(u_ready, n + 1)
                        dve.tensor_tensor(PT.rearrange("p (h c t) -> p h c t", h=2, c=3),
                                          PS[:, 3 * BANK:5 * BANK].rearrange("p (h r) -> p h r", h=2)[:, :, 0:384].rearrange("p h (c t) -> p h c t", c=3),
                                          CM[:, :].unsqueeze(1).unsqueeze(1).broadcast_to([P, 2, 3, P]), ALU.add).then_inc(dm_ready, 1)
                        dve.wait_ge(st_ready, n + 1)
                        dve.wait_ge(pt_ready, n + 1)
                        dve.tensor_tensor(by(WT, 2), PS[:, 5 * BANK:7 * BANK].rearrange("p (h r) -> p h r", h=2)[:, :, 0:384], by(PT, 2), ALU.mult)\
                           .then_inc(w_ready, 1)
                        dve.wait_ge(num_ready, n + 1)
                        c6 = lambda ap: ap.rearrange("p (c h e) -> p c h e", c=3, h=2)
                        dve.tensor_tensor(c6(T1), c6(bank(0, 6 * HB)), per_token(0, g * CG, g * CG + 3, HB), ALU.mult)
                        dve.drain()
                        dve.tensor_tensor(T1, bank(7, 6 * HB), T1, ALU.add)
                        dve.drain()
                        den = c6(T1)[:, :, :, HD:HB].rearrange("p c h e -> p c (h e)")
                        r6 = SMALL[:, 32:38].rearrange("p (c h) -> p c h", c=3)
                        dve.scalar_tensor_tensor(out=r6, in0=den, scalar=-1.0, in1=den, op0=ALU.mult, op1=ALU.max)
                        dve.drain()
                        em = N4[:, :].rearrange("p (c j) -> p c j", c=CH)[:, g * CG:g * CG + 3, bass.ds(2 * p + 16, 2)]
                        dve.tensor_tensor(r6, r6, em, ALU.max)
                        dve.drain()
                        dve.reciprocal(SMALL[:, 32:38], SMALL[:, 32:38])
                        dve.drain()
                        wide = lambda ap: ap.rearrange("p (c h) -> p c h", c=3).unsqueeze(3).broadcast_to([P, 3, 2, HD])
                        dve.tensor_tensor(c6(HBUF), c6(T1)[:, :, :, 0:HD], wide(SMALL[:, 32:38]), ALU.mult)
                        dve.drain()
                        dve.tensor_tensor(SQ, HBUF, HBUF, ALU.mult)
                        dve.drain()
                        dve.tensor_reduce(SMALL[:, 48:54], SQ.rearrange("p (c e) -> p c e", c=6), AX, ALU.add).then_inc(ms_head, 1)
                        dve.wait_ge(rr_ready, n + 1)
                        dve.tensor_tensor(c6(HBUF), c6(HBUF), wide(SMALL[:, 48:54]), ALU.mult).then_inc(hn_ready, 1)
                        dve.wait_ge(ht_ready, n + 1)
                        w = 384 if g < 2 else 256 + DEC
                        dve.scalar_tensor_tensor(out=Y[:, bass.ds(p * T + g * 384, w)], in0=bank(1, w), scalar=GM[:, bass.ds(l * PAIRS + p, 1)],
                                                 in1=OM[:, g * 384:g * 384 + w], op0=ALU.mult, op1=ALU.mult).then_inc(mout_done, 1)

                dve.wait_ge(state_stored, (l + 1) * PAIRS * 128 + 16)
                for i in range(4):
                    s = (1 + i) % 2
                    dve.wait_ge(tile_done, l * TILES + TILE_LATENT + i + 1)
                    dve.tensor_copy(by(X[:, i * T:(i + 1) * T], 3), pset(s)).then_inc(emptied[s], 1)
                for i in range(2):
                    dve.wait_ge(csq_ready, l * 4 + 2 * i + 2)
                    if i == 1:
                        dve.wait_ge(ms_ready, l * NORMS + 2)
                    dve.tensor_tensor(SS[:, :], W2[:, 0:T], W2[:, T:2 * T], ALU.add).then_inc(csq_added, 1)
                    dve.wait_ge(rs_ready, l * NORMS + 2 + i)
                    for j in range(2):
                        t = X[:, (2 * i + j) * T:(2 * i + j + 1) * T]
                        dve.scalar_tensor_tensor(out=t, in0=t, scalar=GC[:, bass.ds(l * 4 + 2 * i + j, 1)], in1=RS[:, :],
                                                 op0=ALU.mult, op1=ALU.mult).then_inc(lat_scaled, 1)
                    for j in range(2):
                        t = X[:, (2 * i + j) * T:(2 * i + j + 1) * T]
                        dst = CQ + j * T if i == 0 else CKV + j * KEYS
                        dve.wait_ge(lat_hi, l * 4 + 2 * i + j + 1)
                        dve.tensor_tensor(HL[:, dst:dst + T], t, HH[:, dst:dst + T], ALU.subtract).then_inc(lat_ready, 1)
                dve.wait_ge(trig_loaded, (l + 1) * 16)
                dve.tensor_tensor(X[64:96, KRF:KRF + T], Y[64:96, KRRAW:KRRAW + T], X[64:96, TRIG:TRIG + T], ALU.mult)
                dve.tensor_tensor(W2[64:96, T:2 * T], Y[96:128, KRRAW:KRRAW + T], X[96:128, TRIG:TRIG + T], ALU.mult)
                dve.drain()
                dve.tensor_tensor(X[64:96, KRF:KRF + T], X[64:96, KRF:KRF + T], W2[64:96, T:2 * T], ALU.add)
                dve.wait_ge(kr_turned, l + 1)
                dve.tensor_copy(X[64:96, KRF + T:KRF + KEYS], PS[0:ROPE, 0:PAST])
                dve.drain()
                dve.memset(SMALL[0:8, 60:61], 0.0).then_inc(kr_full, 1)
                dve.wait_ge(cache_hi, l + 1)
                tail = lambda t: t[:, CKV:CKV + 2 * KEYS].rearrange("p (k c) -> p k c", k=2)[:, :, T:KEYS]
                dve.tensor_tensor(tail(HL), by(PS[:, 3 * BANK:3 * BANK + 2048], 2), tail(HH), ALU.subtract).then_inc(cache_lo, 1)
                for c in range(CH):
                    w = P if c < CH - 1 else DEC
                    dve.wait_ge(nat_turned, l * CH + c + 1)
                    if c >= 3:
                        dve.wait_ge(nat_stored[c % 3], (l * 3 + c // 3) * 32)
                    dve.tensor_copy(Y[0:w, STAGE + c % 3 * 288:STAGE + c % 3 * 288 + 288], bank(c % 2, 288, (0, w))).then_inc(nat_staged, 1)
                dve.wait_ge(krope_hi, l + 1)
                dve.tensor_tensor(HL[64:96, KTO:KTO + KEYS], X[64:96, KRF:KRF + KEYS], HH[64:96, KTO:KTO + KEYS], ALU.subtract)
                dve.memset(HH[96:97, KTO:KTO + KEYS].bitcast(F32), 1.0)
                dve.memset(HL[96:97, KTO:KTO + KEYS].bitcast(F32), 0.0)
                dve.memset(RL[96:97, QTO:QTO + T].bitcast(F32), 0.0)
                dve.memset(RH[:, VO:VO + SEQ].bitcast(F32), 1.0)
                dve.memset(RL[:, VO:VO + SEQ].bitcast(F32), 0.0)
                dve.drain()
                dve.wait_ge(nat_stored[0], (l + 1) * 96)
                dve.wait_ge(nat_stored[1], (l + 1) * 96)
                dve.wait_ge(nat_stored[2], (l + 1) * 96)
                dve.memset(SMALL[0:8, 60:61], 0.0).then_inc(keys_ready, 1)

                with dve.Fori(0, PAIRS) as p:
                    for h in range(2):
                        hd = (l * PAIRS + p) * 2 + h
                        cos, sin = X[64:96, TRIG:TRIG + T], X[96:128, TRIG:TRIG + T]
                        dve.wait_ge(q_proj, hd + 1)
                        dve.tensor_tensor(by(X[64:96, QF:QF + T], 3), pset(0, (64, 96)), by(cos, 3), ALU.mult)
                        dve.tensor_tensor(by(W2[64:96, T:2 * T], 3), pset(0, (96, 128)), by(sin, 3), ALU.mult)
                        dve.drain()
                        dve.wait_ge(qnope_ready, hd + 1)
                        dve.tensor_tensor(X[64:96, QF:QF + T], X[64:96, QF:QF + T], W2[64:96, T:2 * T], ALU.add).then_inc(qf_ready, 1)
                        dve.wait_ge(khi_ready, hd + 1)
                        kvp = PS[:, 3 * BANK:8 * BANK].rearrange("p (n c) -> p n c", n=5)[:, :, 0:416]
                        dve.tensor_tensor(by(HL[0:64, KTO:KTO + KEYS], 5), kvp[0:64], by(HH[0:64, KTO:KTO + KEYS], 5), ALU.subtract).then_inc(qk_ready, 1)
                        dve.wait_ge(qhi_ready, hd + 1)
                        dve.tensor_tensor(RL[0:96, QTO:QTO + T], X[0:96, QF:QF + T], RH[0:96, QTO:QTO + T], ALU.subtract).then_inc(qk_ready, 1)
                        dve.wait_ge(vhi_ready, hd + 1)
                        v8 = lambda t: t[:, VO:VO + SEQ].rearrange("p (t c) -> p t c", t=8)[:, :, 0:HD]
                        dve.tensor_tensor(v8(RL), by(PS[:, 0:512], 8), v8(RH), ALU.subtract)
                        dve.tensor_copy(X[:, VS:VS + 8 * HD], PS[:, 512:1024])
                        dve.tensor_copy(X[0:DEC, VS + 8 * HD:VS + 9 * HD], PS[0:DEC, 1024:1088]).then_inc(v_ready, 1)
                        for i in range(8):
                            b = (3 + 2 * (i % 2)) * BANK
                            dve.wait_ge(smax_ready, hd * 8 + i + 1)
                            dve.tensor_reduce(SMALL[:, i:i + 1], PS[:, b:b + i * P + 64], AX, ALU.max)
                            dve.tensor_reduce(SMALL[64:128, 10 + i:11 + i], PS[64:128, b + i * P + 64:b + (i + 1) * P], AX, ALU.max).then_inc(smax_taken, 1)
                        dve.drain()
                        dve.tensor_tensor(SMALL[64:128, 0:8], SMALL[64:128, 0:8], SMALL[64:128, 10:18], ALU.max).then_inc(max_ready, 1)
                        for b, (kt, q0, q1) in enumerate(BLOCKS):
                            w = q1 - q0
                            f = slice(PF + b % 2 * BANK, PF + b % 2 * BANK + w)
                            r = slice(PO + b % 2 * BANK, PO + b % 2 * BANK + w)
                            dve.wait_ge(p_exp, hd * NB + b + 1)
                            if q0 == kt * P:
                                dve.memset(X[64:128, f.start:f.start + 64], 0.0)
                                dve.drain()
                            if b >= 2:
                                dve.wait_ge(pv_done, hd * NB + b - 1)
                            dve.tensor_copy(RH[:, r], X[:, f])
                            dve.drain()
                            dve.tensor_tensor(RL[:, r], X[:, f], RH[:, r], ALU.subtract).then_inc(p_ready, 1)
                        dve.wait_ge(rden_ready, hd + 1)
                        dve.tensor_tensor(Y[64 * h:64 * h + 64, bass.ds((4 + p) * T, SEQ)], PS[0:64, 6 * BANK:8 * BANK], W2[0:64, 0:SEQ], ALU.mult)\
                           .then_inc(prompt_out, 1)
                        dve.wait_ge(ss_scores, hd + 1)
                        dve.tensor_reduce(SMALL[0:DEC, 20:21], PS[0:DEC, 0:3 * BANK].rearrange("p (n c) -> p n c", n=3)[:, :, 0:TG], mybir.AxisListType.XY, ALU.max)
                        dve.drain()
                        dve.tensor_scalar(SMALL[0:DEC, 21:22], SMALL[0:DEC, 20:21], -SCALE, None, ALU.mult).then_inc(ss_max, 1)
                        dve.wait_ge(ss_exp, hd + 1)
                        dve.reciprocal(SMALL[0:DEC, 23:24], SMALL[0:DEC, 22:23])
                        dve.drain()
                        dve.tensor_scalar(SS[0:DEC, :], SS[0:DEC, :], SMALL[0:DEC, 23:24], None, ALU.mult).then_inc(ss_probs, 1)
                        dve.wait_ge(ss_turned, hd + 1)
                        dve.tensor_copy(X[:, PTS:PTS + 8 * DEC], bank(3, 8 * DEC))
                        dve.tensor_copy(X[0:DEC, PTS + 8 * DEC:PTS + 9 * DEC], bank(3, DEC, (0, DEC), 8 * DEC)).then_inc(ss_pt, 1)
                        dve.wait_ge(ss_pv, hd + 1)
                        dve.tensor_copy(Y[64 * h:64 * h + 64, bass.ds((4 + p) * T + SEQ, DEC)], bank(4, DEC, (0, HD))).then_inc(attn_out, 1)

                for k in range(KT):
                    dve.wait_ge(mix_hi, l * KT + k + 1)
                    dve.tensor_tensor(HL[:, k * T:(k + 1) * T], yt(k), HH[:, k * T:(k + 1) * T], ALU.subtract).then_inc(mix_ready, 1)
                with dve.Fori(0, KT // 2) as m:
                    for i in range(2):
                        dve.wait_ge(tile_done, l * TILES + TILE_OUT + 2 * m + i + 1)
                        dve.tensor_copy(by(Y[:, bass.ds((2 * m + i) * T, T)], 3), pset(i)).then_inc(emptied[i], 1)
                add_squares(l, 1)
                dve.wait_ge(x_back, (l + 1) * 16)
                residual(l, 3, 1, mid_ready)
                dve.drain()
                add_squares(l, 2)
                normed(l, 1, 4)

                dve.memset(Y[:, :], 0.0).then_inc(y_zeroed, 1)

                def inner(g, j, tile, gate_emptied):
                    w, f = slice(j * T, (j + 1) * T), slice(j * T, (j + 1) * T)
                    dve.wait_ge(tile_done, tile + 1)
                    dve.wait_ge(emptied[0], gate_emptied)
                    dve.tensor_tensor(by(W2[:, w], 3), pset(1), by(W2[:, w], 3), ALU.mult).then_inc(emptied[1], 1)
                    dve.drain()
                    dve.tensor_copy(RH[:, f], W2[:, w])
                    dve.drain()
                    dve.tensor_tensor(RL[:, f], W2[:, w], RH[:, f], ALU.subtract).then_inc(ff_ready, 1)

                def outer(tile, s0):
                    for m in range(KT):
                        s = (s0 + m) % 2
                        dve.wait_ge(tile_done, tile + m + 1)
                        dve.tensor_tensor(by(yt(m), 3), pset(s), by(yt(m), 3), ALU.add).then_inc(emptied[s], 1)
                base0 = l * SET_USES[0] + SET_FFN[0] + 1
                with dve.Fori(0, FG - 1) as g:
                    tile = l * TILES + TILE_FFN + 12 * g
                    inner(g, 0, tile + 1, base0 + 6 * g + 1)
                    inner(g, 1, tile + 3, base0 + 6 * g + 2)
                    outer(tile + 5, 1)
                tile = l * TILES + TILE_FFN + 12 * (FG - 1)
                inner(FG - 1, 0, tile + 1, base0 + 6 * (FG - 1) + 1)
                inner(FG - 1, 1, tile + 3, base0 + 6 * (FG - 1) + 2)
                outer(tile + 4, 0)
                dve.drain()
                add_squares(l, 3)
                residual(l, 5, 3, x_ready)
                dve.drain()

            for c in range(CH):
                w = P if c < CH - 1 else DEC
                dve.wait_ge(out_turned, c + 1)
                src = PS[0:w, 2 * (c % 4) * BANK:2 * (c % 4 + 1) * BANK]
                dst = Y[:, c * D:(c + 1) * D] if c < CH - 1 else W2[0:DEC, 0:D]
                dve.tensor_copy(dst, src).then_inc(out_staged, 1)


_INS = ['x_prompt', 'x_sample', 'cache_ckv', 'cache_krope', 'state_mlstm_C', 'state_mlstm_n', 'state_mlstm_m',
        'g_pre_mix', 'g_post_mix', 'g_pre_ffn', 'g_post_ffn', 'w_in', 'b_gates', 'g_mlstm_head',
        'g_q_norm', 'w_uq', 'g_kv_norm', 'w_ukv', 'w_out', 'w_ffn_in', 'w_ffn_out']
_OUTS = [('y_prompt', (1, SEQ, D)), ('y_sample', (1, DEC, D)),
         ('new_ckv_prompt', (LAYERS, 1, SEQ, RANK)), ('new_krope_prompt', (LAYERS, 1, SEQ, ROPE)),
         ('C_prompt', (LAYERS, 1, HEADS, HD, HD)), ('n_prompt', (LAYERS, 1, HEADS, HD)), ('m_prompt', (LAYERS, 1, HEADS)),
         ('new_ckv_sample', (LAYERS, 1, DEC, RANK)), ('new_krope_sample', (LAYERS, 1, DEC, ROPE)),
         ('C_sample', (LAYERS, 1, HEADS, HD, HD)), ('n_sample', (LAYERS, 1, HEADS, HD)), ('m_sample', (LAYERS, 1, HEADS))]


def shape_constants():
    import numpy as np
    t = np.arange(P)
    half = ROPE // 2
    inv = (np.float32(10000.0) ** (-np.arange(half, dtype=np.float32) / np.float32(half))).astype(np.float32)
    ang = (np.arange(T, dtype=np.float32)[None, :] * inv[:, None]).astype(np.float32)
    cos, sin = np.cos(ang), np.sin(ang)
    pair_mask = np.zeros((P, 2 * HB), np.float32)
    pair_mask[:64, :HB] = 1
    pair_mask[64:, HB:] = 1
    select = np.zeros((8, PAIRS, P), np.float32)
    for j in range(PAIRS):
        select[2 * j, j, :64] = 1
        select[2 * j + 1, j, 64:] = 1
    return {
        "identity": np.eye(P, dtype=np.float32),
        "causal": np.where(t[:, None] <= t[None, :], np.float32(0), np.float32(NEG)).astype(np.float32),
        "pair_mask": pair_mask,
        "pair_select": select.reshape(8, PAIRS * P),
        "constants": np.tile(np.array([[EPS, 1.0]], np.float32), (P, 1)),
        "ones": np.ones((P, P), np.float32),
        "zeros": np.zeros((P, 64), np.float32),
        "trig": np.concatenate([cos, cos, -sin, sin], axis=0).astype(np.float32),
    }


def kernel(**inputs):
    import numpy as _np
    import concourse.bacc as _bacc
    from concourse.bass_utils import run_bass_kernel_spmd as _run

    nc = _bacc.Bacc("TRN2", target_bir_lowering=False, num_devices=1)
    arrays, a, o = {}, {}, {}
    for name, value in [(n, inputs[n]) for n in _INS] + list(shape_constants().items()):
        v = _np.ascontiguousarray(value)
        arrays[f"in_{name}"] = v
        a[name] = nc.dram_tensor(f"in_{name}", v.shape, mybir.dt.from_np(v.dtype), kind="ExternalInput").ap()
    for name, shape in _OUTS:
        o[name] = nc.dram_tensor(f"out_{name}", shape, F32, kind="ExternalOutput").ap()
    encoder_step(nc, a, o)
    r = _run(nc, [arrays], core_ids=[0])
    return tuple(r.results[0][f"out_{name}"] for name, _ in _OUTS)
```

```python
from contextlib import ExitStack

import concourse.bass as bass
from concourse import mybir

F32 = mybir.dt.float32
F32R = mybir.dt.float32r
ALU = mybir.AluOpType
ACT = mybir.ActivationFunctionType
AX = mybir.AxisListType.X

P = 128
D = 1024
KT = D // P
SEQ, DEC, PAST = 1024, 32, 1024
T = SEQ + DEC
NG = 3
TG = T // NG
LAYERS = 2
HEADS, HD = 8, 64
PAIRS = HEADS // 2
ROPE = 32
RANK = 256
DFF = 2816
FT = DFF // P
FG = FT // 2
CH = 9
TP = CH * P
CG = 3
KEYS = T + PAST
HB = HD + 1
SLAB = 1024
BANK = 512
EPS = 1e-6
SCALE = float(96) ** -0.5
NEG = -1e30

COL_Q, COL_K, COL_V, COL_O, COL_G = 0, 512, 1024, 1536, 2048
COL_CQ, COL_CKV, COL_KR = 2064, 2320, 2576

SLOT_PAIRS, SLOT_LATENT = (1, 0), (9, 8)
SLOT_HEADS, SLOT_OUT, SLOT_FFN = (11, 10), (15, 10), (19, 14)
RAW_USES = (52, 47)
SPLIT_USES = (41, 36, 22)
FFN_STEPS = ((1, 14), (2, 0), (0, 20), (1, 15), (2, 1), (0, 21))
FFN_LAST = ((1, 34), (2, 20), (0, 40), (1, 35), (2, 21))
PLAIN_0 = 47
SET_PAIRS, SET_OUT, SET_FFN = 1, (21, 0), (25, 4)
SET_USES = (91, 70)
TILES = 161
TILE_PAIRS, TILE_LATENT, TILE_OUT, TILE_FFN = 1, 17, 21, 29
NORMS = 6
SUMS = 2 * (KT - 1) + 2 * KT
SUMS_OF = (0, KT - 1, 2 * KT - 1, 3 * KT - 2, SUMS)
LO_POOL = (1, 3, 5)
LO_DVE = (0, 2, 4, 6, 7)

BLOCKS = []
for _kt in range(SEQ // P):
    if _kt * P < 512:
        BLOCKS.append((_kt, _kt * P, 512))
    BLOCKS.append((_kt, max(512, _kt * P), SEQ))
NB = len(BLOCKS)
MAX_BLOCKS = [(_i, _k, min(_k + BANK, (_i + 1) * P)) for _i in range(SEQ // P) for _k in range(0, (_i + 1) * P, BANK)]
NM = len(MAX_BLOCKS)
PREPARE = {1: ("q",), 2: ("kv0",), 3: ("kv1",), 4: ("v",), 5: ("sample",), 6: ("max0",), 7: ("max1",), 8: ("max2",), 9: ("max3",),
           11: ("mrow",), 12: ("turn",), 13: ("out",)}
STAGES = ("q", "kv0", "kv1", "v", "sample", "max0", "max1", "max2", "max3", "mrow", "turn", "out")


def encoder_step(nc, a, o):
    with ExitStack() as ctx:
        def sb(name, cols, dt=F32, rows=P):
            return ctx.enter_context(nc.sbuf_tensor(name, [rows, cols], dt))

        def sem(name):
            return ctx.enter_context(nc.semaphore(name))

        X = sb("residual", KT * T)
        Y = sb("branch", KT * T)
        HH, HL = sb("act_hi", KT * T, F32R), sb("act_lo", KT * T, F32R)
        RH, RL = sb("small_hi", 3 * SLAB + 64, F32R), sb("small_lo", 3 * SLAB + 64, F32R)
        RAW = sb("slab_raw", 2 * SLAB)
        SH, SL = sb("slab_hi", 2 * SLAB, F32R), sb("slab_lo", 2 * SLAB, F32R)
        W2 = sb("work", 2 * T)
        SS = sb("sum_squares", T)
        RS = sb("rstd", T)
        N4 = sb("gates_by_token", CH * 32)
        UROW = sb("b_minus_m", TP, rows=8)
        IDN = sb("identity", P)
        ONES = sb("ones", P)
        CM = sb("causal", P)
        CONST = sb("constants", 2)
        BM = sb("pair_mask", 2 * HB)
        GN = sb("gains", LAYERS * 4 * KT)
        GM = sb("gain_mlstm", LAYERS * PAIRS)
        GC = sb("gain_latent", LAYERS * 4)
        BG = sb("gate_bias", LAYERS * 3, rows=8)
        SEL = sb("pair_select", PAIRS * P, rows=8)
        DEC_ALL = sb("decay_by_pair", PAIRS * CH)
        SMALL = sb("small", 64)
        PS = ctx.enter_context(nc.psum_tensor("acc", [P, 8 * BANK], F32))
        x_spill = nc.dram_tensor("x_spill", [P, KT * T], F32, kind="Internal").ap()

        def bank(b, w, rows=(0, P), off=0):
            return PS[rows[0]:rows[1], b * BANK + off:b * BANK + off + w]

        def pset(s, rows=(0, P)):
            return PS[rows[0]:rows[1], 3 * s * BANK:3 * (s + 1) * BANK].rearrange("p (n c) -> p n c", n=3)[:, :, 0:TG]

        def by(ap, n):
            return ap.rearrange("p (n c) -> p n c", n=n)

        def slab_parts(slot, c0, c1):
            if slot == 2:
                return RH[:, 2 * T + c0:2 * T + c1], RL[:, 2 * T + c0:2 * T + c1]
            return SH[:, slot * SLAB + c0:slot * SLAB + c1], SL[:, slot * SLAB + c0:slot * SLAB + c1]

        def xt(k):
            return X[:, k * T:(k + 1) * T]

        def yt(k):
            return Y[:, k * T:(k + 1) * T]

        QT, KTT, VT, OM = X[:, 0:TP], X[:, TP:2 * TP], X[:, 2 * TP:3 * TP], X[:, 3 * TP:3 * TP + T]
        KW = X[:, 4 * TP:5 * TP]
        VX = X[:, 5 * TP:5 * TP + CH * 2 * HB]
        C0 = 5 * TP + CH * 2 * HB
        CS = X[:, C0:C0 + 11 * 2 * HB]

        def cs(c, rows=(0, P), cols=(0, 2 * HB)):
            return X[rows[0]:rows[1], C0 + c * 2 * HB + cols[0]:C0 + c * 2 * HB + cols[1]]

        def gt(i, c0=0, c1=TP):
            return Y[0:8, i * TP + c0:i * TP + c1]
        G4 = 5 * TP
        QTS = (QT, Y[:, 4 * T:4 * T + TP])
        KTS = (KTT, Y[:, 4 * T + TP:4 * T + 2 * TP])
        OMS = (OM, RS)
        PTG = (W2[:, 0:6 * P], Y[:, 4 * T + 2 * TP:4 * T + 2 * TP + 6 * P])
        WT = W2[:, 6 * P:12 * P]
        LSQ = (W2[:, 0:T], W2[:, T:2 * T]), (X[:, 4 * T:5 * T], RS[:, :])
        LSUM = SS, X[:, 4 * T:5 * T]
        LRS = RS, W2[:, 0:T]
        T1, UM = W2[:, 12 * P:12 * P + 3 * 2 * HB], Y[0:8, 7 * T:7 * T + 6 * P]
        HBUF, SQ = SS[:, 0:3 * P], SS[:, 3 * P:6 * P]
        CQ, CKV, KTO = 0, 2 * T, 2 * T + 2 * KEYS
        VO, PO = SEQ, 2 * SEQ
        QF, VTF, VS = 0, T, T + KEYS
        PF = VS + 17 * HD
        KRF, TRIG = 5280, 7360
        CACHE = 4 * T
        KRRAW = 7 * T
        KH, KL = (HH[:, KTO:KTO + SEQ], SH[:, SLAB:2 * SLAB]), (HL[:, KTO:KTO + SEQ], SL[:, SLAB:2 * SLAB])
        QH, QL = (RH[:, 0:SEQ], HH[:, KTO + SEQ:KTO + 2 * SEQ]), (RL[:, 0:SEQ], HL[:, KTO + SEQ:KTO + 2 * SEQ])
        KF = X[:, KRF:KRF + KEYS]
        PTS = RS[:, 0:9 * DEC]

        const_loaded, x_loaded = sem("const_loaded"), [sem(f"x_loaded{i}") for i in range(5)]
        raw_landed = [sem("raw_landed0"), sem("raw_landed1")]
        gate_raw_landed, head_raw_landed = sem("gate_raw_landed"), sem("head_raw_landed")
        raw_free = [sem("raw_free0"), sem("raw_free1")]
        slab_ready = [sem(f"slab_ready{i}") for i in range(3)]
        slab_free = [sem(f"slab_free{i}") for i in range(3)]
        tile_done = sem("tile_done")
        emptied = [sem("set_emptied0"), sem("set_emptied1")]
        x_ready, x_spilled, x_back = sem("x_ready"), sem("x_spilled"), sem("x_back")
        in_turned, in_taken = sem("in_turned"), sem("in_taken")
        sq_ready, sq_added = sem("sq_ready"), sem("sq_added")
        csq_ready, csq_added = sem("csq_ready"), sem("csq_added")
        ms_ready, rs_ready = sem("ms_ready"), sem("rs_ready")
        scaled, hi_ready, h_ready, h_ready_pool = sem("scaled"), sem("hi_ready"), sem("h_ready"), sem("h_ready_pool")
        f_ready, softplus_ready, args_ready = sem("f_ready"), sem("softplus_ready"), sem("args_ready")
        gate_exps, gate_turned, gates_ready = sem("gate_exps"), sem("gate_turned"), sem("gates_ready")
        m_stored = sem("m_stored")
        mixer_cleared = sem("mixer_cleared")
        state_loaded, state_stored, states_ready = sem("state_loaded"), sem("state_stored"), sem("states_ready")
        kv_turned, vx_ready, kw_ready, upd_ready = sem("kv_turned"), sem("vx_ready"), sem("kw_ready"), sem("upd_ready")
        um_ready, u_ready, dm_ready, pt_ready = sem("um_ready"), sem("u_ready"), sem("dm_ready"), sem("pt_ready")
        st_ready, w_ready, num_ready = sem("st_ready"), sem("w_ready"), sem("num_ready")
        ms_head, rr_ready, hn_ready, ht_ready = sem("ms_head"), sem("rr_ready"), sem("hn_ready"), sem("ht_ready")
        mout_done = sem("mout_done")
        trig_loaded, cache_loaded = sem("trig_loaded"), sem("cache_loaded")
        lat_scaled, lat_hi, lat_ready = sem("lat_scaled"), sem("lat_hi"), sem("lat_ready")
        cache_turned, cache_hi, cache_lo = sem("cache_turned"), sem("cache_hi"), sem("cache_lo")
        kr_mul, kr_turned, kr_full, krope_hi, keys_ready = sem("kr_mul"), sem("kr_turned"), sem("kr_full"), sem("krope_hi"), sem("keys_ready")
        nat_turned, nat_staged = sem("nat_turned"), sem("nat_staged")
        nat_stored = sem("nat_stored")
        q_proj, kv_proj, qnope_ready, qf_ready = sem("q_proj"), sem("kv_proj"), sem("qnope_ready"), sem("qf_ready")
        qhi_ready, khi_ready, vt_ready, kf_ready = sem("qhi_ready"), sem("khi_ready"), sem("vt_ready"), sem("kf_ready")
        q_split, k_split = sem("q_split"), sem("k_split")
        v_turned, v_staged, vhi_ready, v_ready = sem("v_turned"), sem("v_staged"), sem("vhi_ready"), sem("v_ready")
        smax_ready, smax_taken, max_ready = sem("smax_ready"), sem("smax_taken"), sem("max_ready")
        mrow_turned, mrow_ready = sem("mrow_turned"), sem("mrow_ready")
        s_ready, p_exp, p_hi, p_ready, pv_done = sem("s_ready"), sem("p_exp"), sem("p_hi"), sem("p_ready"), sem("pv_done")
        rden_ready, prompt_out = sem("rden_ready"), sem("prompt_out")
        ss_scores, ss_max, ss_exp, ss_probs = sem("sample_scores"), sem("sample_max"), sem("sample_exp"), sem("sample_probs")
        ss_turned, ss_pt, ss_pv, attn_out = sem("sample_turned"), sem("sample_pt"), sem("sample_pv"), sem("attn_out")
        mid_ready = sem("mid_ready")
        rows_set = sem("rows_set")
        mix_hi, mix_ready = sem("mix_hi"), sem("mix_ready")
        ff_ready = sem("ff_ready")
        out_turned, out_staged = sem("out_turned"), sem("out_staged")
        out_stored = sem("out_stored")

        CONSTS = 16 * 26

        block = ctx.enter_context(nc.Block())

        @block.sync
        def _(sp):
            w_in = a["w_in"].rearrange("l (k p) c -> l p k c", p=P)
            w_fi = a["w_ffn_in"].rearrange("l (k p) c -> l p k c", p=P)
            w_o = a["w_out"].rearrange("l (k p) c -> l p k c", p=P)
            w_uq = a["w_uq"].rearrange("l (k p) (h c) -> l p k h c", p=P, h=HEADS)
            w_ukv = a["w_ukv"].rearrange("l (k p) c -> l p k c", p=P)

            def slab(l, slot, use, source):
                sp.wait_ge(raw_free[slot], l * RAW_USES[slot] + use + 1)
                dst = RAW[:, slot * SLAB:(slot + 1) * SLAB]
                if len(source.shape) == 4:
                    dst, source = dst.rearrange("p (k c) -> p k c", k=KT), source.rearrange("l p k c -> (l p) k c")
                sp.dma_start(dst, source).then_inc(raw_landed[slot], 16)

            with sp.Fori(0, LAYERS) as l:
                one = bass.ds(l, 1)
                sp.wait_ge(raw_free[0], l * RAW_USES[0] + 1)
                g = RAW[:, 0:SLAB].rearrange("p (k c) -> p k c", k=KT)
                for dst, src, n in ((0, COL_G, 8), (32, COL_G + 8, 8), (64, COL_KR, 32), (96, COL_KR + 16, 16), (112, COL_KR, 16)):
                    sp.dma_start(g[:, :, dst:dst + n], w_in[one, :, :, src:src + n].rearrange("l p k c -> (l p) k c")).then_inc(gate_raw_landed, 16)
                with sp.Fori(0, PAIRS) as p:
                    for i, col in enumerate((COL_Q, COL_K, COL_V, COL_O)):
                        slab(l, i % 2, SLOT_PAIRS[i % 2] + 2 * p + i // 2, w_in[one, :, :, bass.ds(p * P + col, P)])
                for i in range(4):
                    slab(l, i % 2, SLOT_LATENT[i % 2] + i // 2, w_in[one, :, :, COL_CQ + i * P:COL_CQ + (i + 1) * P])
                with sp.Fori(0, PAIRS) as p:
                    sp.wait_ge(raw_free[0], l * RAW_USES[0] + SLOT_HEADS[0] + p + 1)
                    hs = RAW[:, 0:SLAB].rearrange("p (k c) -> p k c", k=2)
                    for h in range(2):
                        b = h * 256
                        for dst, src, n in ((0, 0, 96), (96, 80, 16), (112, 64, 16)):
                            sp.dma_start(hs[:, :, b + dst:b + dst + n],
                                         w_uq[one, :, :, bass.ds(2 * p + h, 1), src:src + n].rearrange("l p k h c -> (l p) k (h c)"))\
                              .then_inc(head_raw_landed, 16)
                        sp.dma_start(hs[:, :, b + 128:b + 256],
                                     w_ukv[one, :, :, bass.ds(p * 256 + h * 128, 128)].rearrange("l p k c -> (l p) k c")).then_inc(head_raw_landed, 16)
                with sp.Fori(0, KT // 2) as m:
                    for i in range(2):
                        slab(l, i, SLOT_OUT[i] + m, w_o[one, :, :, bass.ds(m * 256 + i * P, P)])

                def ffn_in(slot, use, tile, up):
                    slab(l, slot, use, w_fi[one, :, :, bass.ds(tile * P + up * DFF, P)])

                def ffn_out(slot, use, tile):
                    slab(l, slot, use, a["w_ffn_out"][one, bass.ds(tile * P, P), :].rearrange("l p c -> (l p) c"))
                u0, u1 = SLOT_FFN
                ffn_in(0, u0, 0, 0)
                with sp.Fori(0, FG - 1) as g_:
                    ffn_in(1, u1 + 3 * g_, 2 * g_, 1)
                    ffn_in(0, u0 + 1 + 3 * g_, 2 * g_ + 1, 0)
                    ffn_in(1, u1 + 1 + 3 * g_, 2 * g_ + 1, 1)
                    ffn_in(0, u0 + 2 + 3 * g_, 2 * g_ + 2, 0)
                    ffn_out(1, u1 + 2 + 3 * g_, 2 * g_)
                    ffn_out(0, u0 + 3 + 3 * g_, 2 * g_ + 1)
                n = 3 * (FG - 1)
                ffn_in(1, u1 + n, FT - 2, 1)
                ffn_in(0, u0 + 1 + n, FT - 1, 0)
                ffn_in(1, u1 + 1 + n, FT - 1, 1)
                ffn_out(0, u0 + 2 + n, FT - 2)
                ffn_out(1, u1 + 2 + n, FT - 1)

        @block.gpsimd
        def _(pool):
            for s in range(2):
                pool.memset(RAW[:, s * SLAB:(s + 1) * SLAB], 0.0).then_inc(raw_free[s], 1)

            pool.wait_ge(const_loaded, CONSTS)

            def split(l, slot, use, landed, count, to=None, to_use=None):
                to, to_use = (slot, use) if to is None else (to, to_use)
                pool.wait_ge(landed, count)
                pool.wait_ge(slab_free[to], l * SPLIT_USES[to] + to_use + 1)
                raw = RAW[:, slot * SLAB:(slot + 1) * SLAB]
                hi, lo = slab_parts(to, 0, SLAB)
                pool.tensor_tensor(hi, raw, ONES[:, 0:1].broadcast_to([P, SLAB]), ALU.mult)
                pool.drain()
                pool.tensor_tensor(lo, raw, hi, ALU.subtract).then_inc(slab_ready[to], 1)
                pool.drain().then_inc(raw_free[slot], 1)

            def plain_split(l, slot, use, skipped=0, to=None, to_use=None):
                per_layer = PLAIN_0 if slot == 0 else RAW_USES[1]
                split(l, slot, use, raw_landed[slot], (l * per_layer + use - skipped + 1) * 16, to, to_use)

            def before_norm(l, i):
                for k in range(1, KT):
                    if k > 1:
                        pool.drain()
                    pool.wait_ge(sq_ready, (l * 4 + 2 * i) * KT + k + 1)
                    pool.tensor_tensor(SS[:, :], W2[:, 0:T] if k == 1 else SS[:, :], W2[:, (k % 2) * T:(k % 2 + 1) * T], ALU.add)\
                        .then_inc(sq_added, 1)
                for k in LO_POOL:
                    pool.wait_ge(hi_ready, (l * 2 + i) * KT + k + 1)
                    pool.tensor_tensor(HL[:, k * T:(k + 1) * T], yt(k), HH[:, k * T:(k + 1) * T], ALU.subtract).then_inc(h_ready_pool, 1)

            with pool.Fori(0, LAYERS) as l:
                split(l, 0, 0, gate_raw_landed, (l + 1) * 16 * 5)
                before_norm(l, 0)
                with pool.Fori(0, PAIRS) as p:
                    for i in range(4):
                        plain_split(l, i % 2, SLOT_PAIRS[i % 2] + 2 * p + i // 2, 1 - i % 2)
                for i in range(4):
                    plain_split(l, i % 2, SLOT_LATENT[i % 2] + i // 2, 1 - i % 2)

                def head_slab(p):
                    split(l, 0, SLOT_HEADS[0] + p, head_raw_landed, (l * PAIRS + p + 1) * 16 * 8)

                def lo_parts(p, h):
                    hd = (l * PAIRS + p) * 2 + h
                    pool.wait_ge(qhi_ready, hd + 1)
                    pool.tensor_tensor(QL[h][0:96], X[0:96, QF:QF + SEQ], QH[h][0:96], ALU.subtract).then_inc(q_split, 1)
                    pool.wait_ge(khi_ready, hd + 1)
                    pool.tensor_tensor(KL[h][0:64], KF[0:64, 0:SEQ], KH[h][0:64], ALU.subtract).then_inc(k_split, 1)
                head_slab(0)
                pool.wait_ge(cache_loaded, (l + 1) * 32)
                pool.wait_ge(tile_done, l * TILES + TILE_OUT)
                pool.wait_ge(trig_loaded, (l + 1) * 16)
                pool.wait_ge(csq_added, l * 2 + 1)
                pool.tensor_tensor(W2[64:128, T:2 * T], Y[64:128, KRRAW:KRRAW + T], X[64:128, TRIG:TRIG + T], ALU.mult).then_inc(kr_mul, 1)
                pool.drain()
                ones = ONES[:, 0:1].broadcast_to([P, SEQ])
                pool.tensor_tensor(RH[:, VO:VO + SEQ], ones, ones, ALU.mult)
                pool.drain()
                pool.memset(RL[:, VO:VO + SEQ].bitcast(F32), 0.0)
                pool.drain()
                for i in range(2):
                    for rows, value in ((KH, 1.0), (KL, 0.0), (QL, 0.0)):
                        pool.memset(rows[i][96:97].bitcast(F32), value)
                pool.drain().then_inc(rows_set, 1)
                lo_parts(0, 0)
                with pool.Fori(0, PAIRS - 1) as p:
                    lo_parts(p, 1)
                    head_slab(p + 1)
                    lo_parts(p + 1, 0)
                lo_parts(PAIRS - 1, 1)
                with pool.Fori(0, KT // 2) as m:
                    for i in range(2):
                        plain_split(l, i, SLOT_OUT[i] + m, 5 if i == 0 else 0)
                u0, u1 = SLOT_FFN
                plain_split(l, 0, u0, 5, 0, u0)
                before_norm(l, 1)
                with pool.Fori(0, FG - 1) as g:
                    for i in range(6):
                        slot = (i + 1) % 2
                        to, use = FFN_STEPS[i]
                        plain_split(l, slot, (u1 if slot else u0 + 1) + 3 * g + i // 2, 0 if slot else 5, to, use + 2 * g)
                for i, (to, use) in enumerate(FFN_LAST):
                    slot = (i + 1) % 2
                    plain_split(l, slot, (u1 if slot else u0 + 1) + 3 * (FG - 1) + i // 2, 0 if slot else 5, to, use)

        @block.tensor
        def _(pe):
            def three(out, wh, wl, xh, xl, first, last):
                pe.matmul(out, wh, xh, start=first, stop=False)
                pe.matmul(out, wl, xh, start=False, stop=False)
                return pe.matmul(out, wh, xl, start=False, stop=last)

            def wait_slab(l, slot, use):
                pe.wait_ge(slab_ready[slot], l * SPLIT_USES[slot] + use + 1)

            def wait_set(l, s, use):
                pe.wait_ge(emptied[s], l * SET_USES[s] + use + 1)

            def product_step(l, slot, slot_use, s, set_use, k, frees=()):
                frees = list(frees)
                if k == 0:
                    wait_slab(l, slot, slot_use)
                    wait_set(l, s, set_use)
                wh, wl = slab_parts(slot, k * P, (k + 1) * P)
                for n in range(NG):
                    x = slice(k * T + n * TG, k * T + (n + 1) * TG)
                    out = bank(3 * s + n, TG)
                    mm = pe.matmul(out, wh, HH[:, x], start=k == 0, stop=False)
                    if k == 0 and frees:
                        mm.then_inc(slab_free[frees.pop(0)], 1)
                    pe.matmul(out, wl, HH[:, x], start=False, stop=False)
                    mm = pe.matmul(out, wh, HL[:, x], start=False, stop=k == KT - 1)
                return mm

            def product(l, slot, slot_use, s, set_use, frees=(), ready=None):
                for k in range(KT):
                    if ready is not None:
                        ready(k)
                    mm = product_step(l, slot, slot_use, s, set_use, k, frees)
                return mm

            def h_tile(l, i):
                def wait(k):
                    if k in LO_POOL:
                        pe.wait_ge(h_ready_pool, (l * 2 + i) * len(LO_POOL) + LO_POOL.index(k) + 1)
                    else:
                        pe.wait_ge(h_ready, (l * 2 + i) * len(LO_DVE) + LO_DVE.index(k) + 1)
                return wait

            def mean_square(l, i, summed, count, total=SS):
                pe.wait_ge(summed, count)
                for n in range(NG):
                    mm = pe.matmul(bank(n, TG), ONES[:, :], total[:, n * TG:(n + 1) * TG], start=True, stop=True)
                mm.then_inc(ms_ready, 1)

            pe.wait_ge(const_loaded, CONSTS)
            for c in range(CH):
                w = P if c < CH - 1 else DEC
                pe.wait_ge(x_loaded[c // 2], 16)
                if c >= 4:
                    pe.wait_ge(in_taken, c - 3)
                for k in range(KT):
                    src = Y[:, c * D + k * P:c * D + (k + 1) * P] if c < CH - 1 else W2[0:DEC, k * P:(k + 1) * P]
                    mm = pe.transpose(bank(2 * (c % 4), w, off=k * P), src, IDN[0:w, 0:w])
                mm.then_inc(in_turned, 1)
            pe.wait_ge(in_taken, CH)

            with pe.Fori(0, LAYERS) as l:
                mean_square(l, 0, sq_added, l * SUMS + SUMS_OF[1])
                mm = product(l, 0, 0, 0, 0, ready=h_tile(l, 0))
                mm.then_inc(tile_done, 1)
                pe.drain().then_inc(slab_free[0], 1)
                def fill(p, a, b):
                    for t in range(a, b):
                        i, k = t // KT, t % KT
                        mm = product_step(l, i % 2, SLOT_PAIRS[i % 2] + 2 * p + i // 2, 0, SET_PAIRS + 4 * p + i, k,
                                          frees=(1 - i % 2,) if i else ())
                        if k == KT - 1:
                            mm.then_inc(tile_done, 1)

                def mlstm(p, par, free_last=True):
                    u = l * PAIRS + p
                    pe.wait_ge(mout_done, u * 3 + 1)
                    wait_set(l, 0, SET_PAIRS + 4 * p + 3)
                    pe.wait_ge(mixer_cleared, l + 1)
                    last = slice((CH - 1) * P, CH * P)
                    for c in range(CH - 1):
                        pe.transpose(PS[:, 3 * BANK + c * P:3 * BANK + (c + 1) * P], VT[:, c * P:(c + 1) * P], IDN[:, :])
                    pe.transpose(bank(7, P), VT[:, last], IDN[:, :])
                    pe.transpose(bank(7, P, off=P), KTS[par][:, last], IDN[:, :]).then_inc(kv_turned, 1)
                    for c in range(CH - 1):
                        mm = pe.transpose(PS[:, 5 * BANK + c * P:5 * BANK + (c + 1) * P], KTS[par][:, c * P:(c + 1) * P], IDN[:, :])
                    mm.then_inc(kv_turned, 1)
                    fill(p + 1, 0, 3)
                    pe.wait_ge(vx_ready, u + 1)
                    pe.wait_ge(kw_ready, u + 1)
                    for c in range(CH):
                        mm = pe.matmul(bank(3 + c // CG, 2 * HB, off=c % CG * 2 * HB), KW[:, c * P:(c + 1) * P],
                                       VX[:, c * 2 * HB:(c + 1) * 2 * HB], start=True, stop=True)
                    mm.then_inc(upd_ready, 1)
                    fill(p + 1, 3, 6)

                    def u_rows(g):
                        pe.wait_ge(um_ready, u * 3 + g + 1)
                        for h in range(2):
                            mm = pe.matmul(bank(3 + h, 3 * P), ONES[0:8, :], UM[0:8, h * 384:(h + 1) * 384], start=True, stop=True)
                        mm.then_inc(u_ready, 1)
                    pe.wait_ge(states_ready, u + 1)
                    u_rows(0)
                    for g in range(3):
                        n = u * 3 + g
                        if g:
                            pe.wait_ge(mout_done, n + 1)
                        for h in range(2):
                            r = slice(64 * h, 64 * h + 64)
                            for c in range(CG):
                                t = slice((g * CG + c) * P, (g * CG + c + 1) * P)
                                mm = pe.matmul(bank(5 + h, P, off=c * P), KTS[par][r, t], QTS[par][r, t], start=True, stop=True)
                        mm.then_inc(st_ready, 1)
                        f = 6 + 8 * g
                        fill(p + 1, f, f + 2)
                        if g < 2:
                            pe.wait_ge(dm_ready, n + 1)
                            u_rows(g + 1)
                        fill(p + 1, f + 2, f + 4)
                        pe.wait_ge(w_ready, n + 1)
                        for c in range(CG):
                            t = (g * CG + c) * P
                            state = cs(g * CG + c) if g * CG + c < CH - 1 else cs(10)
                            mm = pe.matmul(bank(5, 2 * HB, off=c * 2 * HB), QTS[par][:, t:t + P], state, start=True, stop=True)
                        for h in range(2):
                            for c in range(CG):
                                j = (g * CG + c) * 2 * HB + h * HB
                                mm = pe.matmul(bank(7, HB, off=(2 * c + h) * HB), WT[:, (3 * h + c) * P:(3 * h + c + 1) * P],
                                               VX[:, j:j + HB], start=True, stop=True)
                        mm.then_inc(num_ready, 1)
                        fill(p + 1, f + 4, f + 8)
                        pe.wait_ge(hn_ready, n + 1)
                        for c in range(CG):
                            mm = pe.transpose(bank(6, P, off=c * P), HBUF[:, c * P:(c + 1) * P], IDN[:, :])
                        mm.then_inc(ht_ready, 1)
                    fill(p + 1, 30, 32)
                    if free_last:
                        pe.drain().then_inc(slab_free[1], 1)
                fill(0, 0, 2 * KT)
                pe.wait_ge(gate_exps, l * 4 + 4)
                for c in range(CH):
                    mm = pe.transpose(PS[:, 3 * BANK + c * P:3 * BANK + (c + 1) * P], X[:, G4 + c * P:G4 + (c + 1) * P], IDN[:, :])
                for j in range(PAIRS):
                    mm = pe.matmul(bank(6, CH, off=j * CH), SEL[:, j * P:(j + 1) * P], SMALL[0:8, 40:40 + CH], start=True, stop=True)
                mm.then_inc(gate_turned, 1)
                fill(0, 2 * KT, 4 * KT)
                pe.drain().then_inc(slab_free[1], 1)
                pe.wait_ge(gates_ready, l + 1)
                mlstm(0, 0)
                with pe.Fori(0, PAIRS // 2 - 1) as i:
                    mlstm(2 * i + 1, 1)
                    mlstm(2 * i + 2, 0)
                mlstm(PAIRS - 1, 1, free_last=False)

                pe.wait_ge(mout_done, l * PAIRS * 3 + PAIRS * 3 + 1)
                mean_square(l, 1, csq_added, l * 2 + 1)
                pe.wait_ge(cache_loaded, (l + 1) * 32)
                for kt in range(2):
                    for t in range(8):
                        mm = pe.transpose(PS[:, 3 * BANK + (kt * 8 + t) * P:3 * BANK + (kt * 8 + t + 1) * P],
                                          Y[:, CACHE + t * 256 + kt * P:CACHE + t * 256 + (kt + 1) * P], IDN[:, :])
                mm.then_inc(cache_turned, 1)
                pe.wait_ge(rs_ready, l * NORMS + 2)
                mean_square(l, 2, csq_added, l * 2 + 2, LSUM[1])
                pe.wait_ge(rs_ready, l * NORMS + 3)
                for t in range(8):
                    mm = pe.transpose(PS[0:ROPE, t * P:(t + 1) * P], Y[:, CACHE + 2048 + t * ROPE:CACHE + 2048 + (t + 1) * ROPE], IDN[:, :])
                mm.then_inc(kr_turned, 1)

                def natural_rows():
                    pe.wait_ge(lat_scaled, l * 4 + 4)
                    pe.wait_ge(cache_lo, l + 1)
                    for c in range(CH):
                        w = P if c < CH - 1 else DEC
                        b = 3 + c % 5
                        if c >= 5:
                            pe.wait_ge(nat_staged, l * CH + c - 4)
                        for j in range(2):
                            pe.transpose(bank(b, P, (0, w), j * P), X[:, (2 + j) * T + c * P:(2 + j) * T + c * P + w], IDN[:, :])
                        pe.transpose(bank(b, ROPE, (0, w), 2 * P), X[64:96, KRF + c * P:KRF + c * P + w], IDN[64:96, 64:96])\
                            .then_inc(nat_turned, 1)

                def prepare(p, h, stage):
                    hd = (l * PAIRS + p) * 2 + h
                    if stage == "q":
                        if h == 0:
                            wait_slab(l, 0, SLOT_HEADS[0] + p)
                        pe.wait_ge(attn_out, hd + 1)
                        for n in range(NG):
                            for k in range(2):
                                w = slice(k * 512 + h * 256, k * 512 + h * 256 + P)
                                x = slice(CQ + k * T + n * TG, CQ + k * T + (n + 1) * TG)
                                mm = three(bank(n, TG), SH[:, w], SL[:, w], HH[:, x], HL[:, x], k == 0, k == 1)
                        mm.then_inc(q_proj, 1)
                    elif stage in ("kv0", "kv1"):
                        r = int(stage[2])
                        if r == 0:
                            pe.wait_ge(qf_ready, hd + 1)
                        else:
                            pe.wait_ge(vt_ready, hd * 2 + 1)
                            pe.wait_ge(kf_ready, hd * 2 + 1)
                        for n in range(3 * r, min(3 * r + 3, 5)):
                            for k in range(2):
                                w = slice(k * 512 + h * 256 + P, k * 512 + h * 256 + 2 * P)
                                x = slice(CKV + k * KEYS + n * 416, CKV + k * KEYS + (n + 1) * 416)
                                mm = three(bank(n - 3 * r, 416), SH[:, w], SL[:, w], HH[:, x], HL[:, x], k == 0, k == 1)
                        mm.then_inc(kv_proj, 1)
                        if h == 1 and r == 1:
                            pe.drain().then_inc(slab_free[0], 1)
                    elif stage == "v":
                        pe.wait_ge(vt_ready, hd * 2 + 2)
                        pe.wait_ge(kf_ready, hd * 2 + 2)
                        for t in range(17):
                            k0, w = (t * P, P) if t < 8 else (T + (t - 8) * P, P) if t < 16 else (SEQ, DEC)
                            out, src = PS[0:w, t * HD:(t + 1) * HD], X[64:128, VTF + k0:VTF + k0 + w]
                            if t == 0:
                                pe.matmul(out, src, IDN[64:128, 64:128], start=True, stop=True)
                            else:
                                mm = pe.transpose(out, src, IDN[64:128, 64:128])
                        mm.then_inc(v_turned, 1)
                    elif stage == "sample":
                        pe.wait_ge(v_staged, hd + 1)
                        for n in range(NG):
                            mm = pe.matmul(bank(n, TG, (0, DEC)), X[0:96, QF + SEQ:QF + T], KF[0:96, SEQ + n * TG:SEQ + (n + 1) * TG],
                                           start=True, stop=True)
                        mm.then_inc(ss_scores, 1)
                    elif stage[:3] == "max":
                        for j in range(3 * int(stage[3]), 3 * int(stage[3]) + 3):
                            i, k0, k1 = MAX_BLOCKS[j]
                            if j == 0:
                                pe.wait_ge(ss_exp, hd + 1)
                                pe.wait_ge(qhi_ready, hd + 1)
                                pe.wait_ge(khi_ready, hd + 1)
                            if j >= 3:
                                pe.wait_ge(smax_taken, hd * NM + j - 2)
                            pe.matmul(bank(j % 3, k1 - k0), QH[h][0:96, i * P:(i + 1) * P], KH[h][0:96, k0:k1], start=True, stop=True)\
                              .then_inc(smax_ready, 1)
                    elif stage == "turn":
                        pe.wait_ge(ss_probs, hd + 1)
                        pe.wait_ge(smax_taken, (hd + 1) * NM)
                        for t in range(8):
                            out, src = bank(0, DEC, off=t * DEC), SS[0:DEC, DEC + t * P:DEC + (t + 1) * P]
                            if t == 0:
                                pe.matmul(out, src, IDN[0:DEC, 0:DEC], start=True, stop=True)
                            else:
                                pe.transpose(out, src, IDN[0:DEC, 0:DEC])
                        pe.transpose(bank(0, DEC, (0, DEC), 8 * DEC), SS[0:DEC, 0:DEC], IDN[0:DEC, 0:DEC]).then_inc(ss_turned, 1)
                    elif stage == "mrow":
                        pe.wait_ge(max_ready, hd + 1)
                        for i in range(8):
                            mm = pe.matmul(PS[0:1, BANK + i * P:BANK + (i + 1) * P], SMALL[:, i:i + 1], IDN[:, :], start=True, stop=True)
                        mm.then_inc(mrow_turned, 1)
                    else:
                        pe.wait_ge(ss_pt, hd + 1)
                        for t in range(9):
                            w = P if t < 8 else DEC
                            v = VS + (8 + t) * HD
                            mm = pe.matmul(bank(0, DEC, (0, HD), 9 * DEC), X[0:w, v:v + HD], PTS[0:w, t * DEC:(t + 1) * DEC],
                                           start=t == 0, stop=t == 8)
                        mm.then_inc(ss_pv, 1)

                def attend(p, h, np, nh):
                    hd = (l * PAIRS + p) * 2 + h
                    pe.wait_ge(mrow_ready, hd + 1)
                    pe.wait_ge(q_split, hd + 1)
                    pe.wait_ge(k_split, hd + 1)
                    pe.wait_ge(p_exp, hd * NB)
                    for b in range(NB + 2):
                        if b < NB:
                            kt, q0, q1 = BLOCKS[b]
                            if b >= 3:
                                pe.wait_ge(p_exp, hd * NB + b - 2)
                            k, q = slice(kt * P, (kt + 1) * P), slice(q0, q1)
                            three(bank(3 + b % 3, q1 - q0), KH[h][0:97, k], KL[h][0:97, k], QH[h][0:97, q], QL[h][0:97, q], True, True)\
                                .then_inc(s_ready, 1)
                        if b >= 2:
                            kt, q0, q1 = BLOCKS[b - 2]
                            w = q1 - q0
                            out = PS[:, 6 * BANK + q0:6 * BANK + q1]
                            par = (b - 2) % 2 * BANK
                            v, pr = slice(VO + kt * P, VO + (kt + 1) * P), slice(PO + par, PO + par + w)
                            if b == 2:
                                pe.wait_ge(v_ready, hd + 1)
                                pe.wait_ge(prompt_out, hd)
                            pe.wait_ge(p_ready, hd * NB + b - 1)
                            first, last = kt == 0, kt == (3 if q0 < 512 else 7)
                            pe.matmul(out, RH[:, v], RH[:, pr], start=first, stop=False)
                            pe.matmul(out, RL[:, v], RH[:, pr], start=False, stop=False)
                            pe.matmul(out, RH[:, v], RL[:, pr], start=False, stop=last).then_inc(pv_done, 1)
                        if np is not None:
                            for stage in PREPARE.get(b, ()):
                                prepare(np, nh, stage)

                pe.wait_ge(kr_full, l + 1)
                pe.wait_ge(lat_ready, l * 4 + 2)
                prepare(0, 0, "q")
                natural_rows()
                pe.wait_ge(lat_ready, l * 4 + 4)
                for stage in STAGES[1:]:
                    if stage == "v":
                        pe.wait_ge(nat_staged, l * CH + CH)
                    if stage == "max0":
                        pe.wait_ge(keys_ready, l + 1)
                    prepare(0, 0, stage)
                pe.wait_ge(rows_set, l + 1)
                attend(0, 0, 0, 1)
                with pe.Fori(0, PAIRS - 1) as p:
                    attend(p, 1, p + 1, 0)
                    attend(p + 1, 0, p + 1, 1)
                attend(PAIRS - 1, 1, None, None)
                pe.drain().then_inc(slab_free[1], 1)

                with pe.Fori(0, KT // 2) as m:
                    product(l, 0, SLOT_OUT[0] + m, 0, SET_OUT[0] + m, ready=lambda k: pe.wait_ge(mix_ready, l * KT + k + 1)).then_inc(tile_done, 1)
                    product(l, 1, SLOT_OUT[1] + m, 1, SET_OUT[1] + m, frees=(0,)).then_inc(tile_done, 1)
                    pe.drain().then_inc(slab_free[1], 1)
                mean_square(l, 3, sq_added, l * SUMS + SUMS_OF[2])
                mean_square(l, 4, sq_added, l * SUMS + SUMS_OF[3])

                def inner(step, s, set_use, frees, ready=None):
                    slot, use = step
                    product(l, slot, use, s, set_use, frees, ready).then_inc(tile_done, 1)

                def outer(g, slots, s0, set_uses, frees):
                    for slot, use in slots:
                        wait_slab(l, slot, use)
                    pe.wait_ge(ff_ready, (l * FG + g + 1) * 2)
                    for m in range(KT):
                        s = (s0 + m) % 2
                        wait_set(l, s, set_uses[s] + m // 2)
                        for j in range(2):
                            wh, wl = slab_parts(slots[j][0], m * P, (m + 1) * P)
                            for n in range(NG):
                                x = slice(j * T + n * TG, j * T + (n + 1) * TG)
                                out = bank(3 * s + n, TG)
                                mm = pe.matmul(out, wh, RH[:, x], start=j == 0, stop=False)
                                if m == j == n == 0:
                                    mm.then_inc(slab_free[frees], 1)
                                pe.matmul(out, wl, RH[:, x], start=False, stop=False)
                                mm = pe.matmul(out, wh, RL[:, x], start=False, stop=j == 1)
                        mm.then_inc(tile_done, 1)
                    for slot, _ in slots:
                        pe.drain().then_inc(slab_free[slot], 1)

                s0, s1 = SET_FFN
                inner((0, SLOT_FFN[0]), 0, s0, (), h_tile(l, 1))
                pe.drain().then_inc(slab_free[0], 1)
                with pe.Fori(0, FG - 1) as g:
                    step = [(slot, use + 2 * g) for slot, use in FFN_STEPS]
                    inner(step[0], 1, s1 + 6 * g, ())
                    inner(step[1], 0, s0 + 1 + 6 * g, (1,))
                    inner(step[2], 1, s1 + 1 + 6 * g, (2,))
                    inner(step[3], 0, s0 + 2 + 6 * g, (0,))
                    outer(g, step[4:6], 1, (s0 + 3 + 6 * g, s1 + 2 + 6 * g), 1)
                n6 = 6 * (FG - 1)
                inner(FFN_LAST[0], 1, s1 + n6, ())
                inner(FFN_LAST[1], 0, s0 + 1 + n6, (1,))
                inner(FFN_LAST[2], 1, s1 + 1 + n6, (2,))
                outer(FG - 1, FFN_LAST[3:5], 0, (s0 + 2 + n6, s1 + 2 + n6), 0)
                mean_square(l, 5, sq_added, l * SUMS + SUMS_OF[4])

            pe.wait_ge(x_ready, (LAYERS + 1) * KT)
            for c in range(CH):
                w = P if c < CH - 1 else DEC
                if c >= 4:
                    pe.wait_ge(out_staged, c - 3)
                for k in range(KT):
                    mm = pe.transpose(bank(2 * (c % 4), P, (0, w), k * P), X[:, k * T + c * P:k * T + c * P + w], IDN[:, :])
                mm.then_inc(out_turned, 1)

        @block.scalar
        def _(act):
            def square(l, i, k, src):
                act.activation(W2[:, (k % 2) * T:(k % 2 + 1) * T], src, ACT.Square).then_inc(sq_ready, 1)

            def squares_of_x(l, i, ready):
                for k in range(KT):
                    act.wait_ge(ready, l * KT + k + 1)
                    if k >= 2:
                        act.wait_ge(sq_added, l * SUMS + SUMS_OF[i] + max(k - 2, 1))
                    square(l, i, k, xt(k))

            def rstd(l, i, width, out=RS):
                act.wait_ge(ms_ready, l * NORMS + i + 1)
                act.activation(by(out[:, 0:T], 3), pset(0), ACT.Ln, bias=CONST[:, 0:1], scale=1.0 / width)
                act.drain()
                act.activation(out[:, 0:T], out[:, 0:T], ACT.Exp, scale=-0.5).then_inc(rs_ready, 1)

            def hi_of_h(l, i):
                for k in range(KT):
                    act.wait_ge(scaled, l * 2 * KT + i * KT + k + 1)
                    act.activation(HH[:, k * T:(k + 1) * T], yt(k), ACT.Copy).then_inc(hi_ready, 1)

            act.dma_start(IDN[:, :], a["identity"]).then_inc(const_loaded, 16)
            act.dma_start(CM[:, :], a["causal"]).then_inc(const_loaded, 16)
            act.dma_start(BM[:, :], a["pair_mask"]).then_inc(const_loaded, 16)
            act.dma_start(SEL[:, :], a["pair_select"]).then_inc(const_loaded, 16)
            act.dma_start(CONST[:, :], a["constants"]).then_inc(const_loaded, 16)
            for c in range(0, CH - 1, 2):
                act.dma_start(Y[:, c * D:(c + 2) * D].rearrange("p (c d) -> p c d", c=2),
                              a["x_prompt"][0, c * P:(c + 2) * P, :].rearrange("(c p) d -> p c d", p=P)).then_inc(x_loaded[c // 2], 16)
            act.dma_start(W2[0:DEC, 0:D], a["x_sample"][0, :, :]).then_inc(x_loaded[4], 16)
            with nc.allow_non_contiguous_dma("gains, once"):
                for i, name in enumerate(("g_pre_mix", "g_post_mix", "g_pre_ffn", "g_post_ffn")):
                    for j in range(LAYERS):
                        act.dma_start(GN[:, (j * 4 + i) * KT:(j * 4 + i + 1) * KT], a[name][j, :].rearrange("(k p) -> p k", p=P),
                                      allow_slow_non_contiguous=True).then_inc(const_loaded, 16)
                act.dma_start(by(GM[:, :], LAYERS), a["g_mlstm_head"].rearrange("l (k p) -> p l k", p=P),
                              allow_slow_non_contiguous=True).then_inc(const_loaded, 16)
                for j in range(LAYERS):
                    act.dma_start(GC[:, 4 * j:4 * j + 2], a["g_q_norm"][j, :].rearrange("(k p) -> p k", p=P),
                                  allow_slow_non_contiguous=True).then_inc(const_loaded, 16)
                    act.dma_start(GC[:, 4 * j + 2:4 * j + 4], a["g_kv_norm"][j, :].rearrange("(k p) -> p k", p=P),
                                  allow_slow_non_contiguous=True).then_inc(const_loaded, 16)
                for j in range(LAYERS):
                    for c in range(2):
                        act.dma_start(BG[:, 3 * j + c:3 * j + c + 1], a["b_gates"][j, c * HEADS:(c + 1) * HEADS].unsqueeze(1),
                                      allow_slow_non_contiguous=True).then_inc(const_loaded, 16)
                    act.dma_start(BG[:, 3 * j + 2:3 * j + 3], a["state_mlstm_m"][j, 0, :].unsqueeze(1),
                                  allow_slow_non_contiguous=True).then_inc(const_loaded, 16)
                act.dma_start(ONES[:, :], a["ones"]).then_inc(const_loaded, 16)
                act.dma_start(SMALL[:, :], a["zeros"]).then_inc(const_loaded, 16)
            act.wait_ge(const_loaded, CONSTS)

            with act.Fori(0, LAYERS) as l:
                one = bass.ds(l, 1)
                act.preload_act_table_set("natural_log_exp_and_others")
                squares_of_x(l, 0, x_ready)
                act.dma_start(x_spill, X[:, :]).then_inc(x_spilled, 16)
                rstd(l, 0, D)
                hi_of_h(l, 0)
                def fill(p, par, a, b):
                    for i in range(a // KT, b // KT):
                        act.wait_ge(tile_done, l * TILES + TILE_PAIRS + 4 * p + i + 1)
                        if isinstance(p, int) and p == PAIRS:
                            dst, func, scale = X[:, i * T:(i + 1) * T], ACT.Copy, 1.0
                        else:
                            dst, func, scale = ((QTS[par], ACT.Copy, 1.0), (KTS[par], ACT.Copy, HD ** -0.5), (VT, ACT.Copy, 1.0),
                                                (OMS[par], ACT.Sigmoid, 1.0))[i]
                        act.activation(by(dst[:, 0:T], 3), pset(0), func, scale=scale).then_inc(emptied[0], 1)

                act.wait_ge(f_ready, l + 1)
                act.activation(gt(3, 0, T), gt(2, 0, T), ACT.Exp)
                act.drain()
                act.activation(gt(3, 0, T), gt(3, 0, T), ACT.Ln, bias=CONST[0:8, 1:2]).then_inc(softplus_ready, 1)
                act.wait_ge(x_spilled, (l + 1) * 16)
                fill(0, 0, 0, KT)
                act.wait_ge(args_ready, l + 1)
                act.activation(SMALL[0:8, 40:40 + CH], SMALL[0:8, 30:30 + CH], ACT.Exp)
                act.activation(X[0:8, G4:G4 + TP], gt(1), ACT.Exp).then_inc(gate_exps, 1)
                act.activation(X[32:40, G4:G4 + TP], gt(4), ACT.Exp).then_inc(gate_exps, 1)
                act.activation(X[64:72, G4:G4 + TP], gt(2), ACT.Exp, scale=-1.0).then_inc(gate_exps, 1)
                act.activation(X[96:104, G4:G4 + TP], gt(0), ACT.Copy).then_inc(gate_exps, 1)
                with nc.allow_non_contiguous_dma("last m of each head"):
                    act.dma_start(o["m_prompt"][one, 0, :].rearrange("l h -> h l"), SMALL[0:8, 7:8], allow_slow_non_contiguous=True).then_inc(m_stored, 16)
                    act.dma_start(o["m_sample"][one, 0, :].rearrange("l h -> h l"), SMALL[0:8, 8:9], allow_slow_non_contiguous=True).then_inc(m_stored, 16)

                def mlstm(p, par, store=True):
                    u = l * PAIRS + p
                    act.preload_act_table_set("natural_log_exp_and_others")
                    act.wait_ge(kv_turned, u * 2 + 1)
                    act.wait_ge(mixer_cleared, l + 1)
                    vx = VX.rearrange("p (c h e) -> p c h e", c=CH, h=2)[:, :, :, 0:HD]
                    act.activation(vx[:, CH - 1:CH], bank(7, P).rearrange("p (c h e) -> p c h e", c=1, h=2), ACT.Copy)
                    act.activation(vx[:, 0:CH - 1], PS[:, 3 * BANK:5 * BANK].rearrange("p (c h e) -> p c h e", c=CH - 1, h=2), ACT.Copy).then_inc(vx_ready, 1)
                    act.wait_ge(state_stored, u * 128 + 16)
                    for h in range(2):
                        r, j = (64 * h, 64 * h + 64), HB * h
                        act.dma_start(cs(10, r, (j, j + HD)), a["state_mlstm_C"][one, 0, bass.ds(2 * p + h, 1), :, :].rearrange("l h d e -> (l h d) e"))\
                           .then_inc(state_loaded, 16)
                        act.dma_start(cs(10, r, (j + HD, j + HB)), a["state_mlstm_n"][one, 0, bass.ds(2 * p + h, 1), :].rearrange("l h d -> (l h d)").unsqueeze(1))\
                           .then_inc(state_loaded, 16)

                    def exps(g):
                        act.wait_ge(dm_ready, u * 3 + g + 1)
                        for h in range(2):
                            for c in range(CG):
                                q = PTG[g % 2][:, (3 * h + c) * P:(3 * h + c + 1) * P]
                                j = (g * CG + c) * 32 + 24 + h
                                bias = N4[:, j + 2 * p:j + 2 * p + 1] if isinstance(p, int) else N4[:, bass.ds(j + 2 * p, 1)]
                                e = act.activation(q, q, ACT.Exp, bias=bias)
                        e.then_inc(pt_ready, 1)
                    exps(0)
                    for g in range(3):
                        n = u * 3 + g
                        f = 6 + 8 * g
                        fill(p + 1, 1 - par, f, f + 4)
                        if g < 2:
                            exps(g + 1)
                        act.wait_ge(ms_head, n + 1)
                        act.activation(SMALL[:, 48:54], SMALL[:, 48:54], ACT.Ln, bias=CONST[:, 0:1], scale=1.0 / HD)
                        act.drain()
                        act.activation(SMALL[:, 48:54], SMALL[:, 48:54], ACT.Exp, scale=-0.5).then_inc(rr_ready, 1)
                        fill(p + 1, 1 - par, f + 4, f + 8)
                    fill(p + 1, 1 - par, 30, 32)
                    if store:
                        store_states(p)

                def store_states(p):
                    for cn, nn, c in (("C_prompt", "n_prompt", 8), ("C_sample", "n_sample", 9)):
                        for h in range(2):
                            r, j = (64 * h, 64 * h + 64), HB * h
                            act.dma_start(o[cn][one, 0, bass.ds(2 * p + h, 1), :, :].rearrange("l h d e -> (l h d) e"), cs(c, r, (j, j + HD)))\
                               .then_inc(state_stored, 16)
                            act.dma_start(o[nn][one, 0, bass.ds(2 * p + h, 1), :].rearrange("l h d -> (l h d)").unsqueeze(1), cs(c, r, (j + HD, j + HB)))\
                               .then_inc(state_stored, 16)
                fill(0, 0, KT, 4 * KT)
                mlstm(0, 0)
                with act.Fori(0, PAIRS // 2 - 1) as i:
                    mlstm(2 * i + 1, 1)
                    mlstm(2 * i + 2, 0)
                mlstm(PAIRS - 1, 1, store=False)

                act.wait_ge(mout_done, (l + 1) * PAIRS * 3 + 1)
                act.dma_start(Y[:, CACHE:CACHE + 2048].rearrange("p (t c) -> p t c", t=8),
                              a["cache_ckv"][one, 0, :, :].rearrange("l (t p) c -> p (l t) c", p=P)).then_inc(cache_loaded, 16)
                act.dma_start(Y[:, CACHE + 2048:CACHE + 2304].rearrange("p (t c) -> p t c", t=8),
                              a["cache_krope"][one, 0, :, :].rearrange("l (t p) c -> p (l t) c", p=P)).then_inc(cache_loaded, 16)
                act.drain()
                for i in range(2):
                    for j in range(2):
                        act.activation(LSQ[i][j], X[:, (2 * i + j) * T:(2 * i + j + 1) * T], ACT.Square).then_inc(csq_ready, 1)
                store_states(PAIRS - 1)
                act.wait_ge(state_stored, (l + 1) * PAIRS * 128 + 16)
                act.dma_start(X[64:128, TRIG:TRIG + T], a["trig"]).then_inc(trig_loaded, 16)
                act.wait_ge(csq_added, l * 2 + 2)
                for i in range(2):
                    rstd(l, 1 + i, RANK, LRS[i])
                    for j in range(2):
                        act.wait_ge(lat_scaled, l * 4 + 2 * i + j + 1)
                        dst = CQ + j * T if i == 0 else CKV + j * KEYS
                        act.activation(HH[:, dst:dst + T], X[:, (2 * i + j) * T:(2 * i + j + 1) * T], ACT.Copy).then_inc(lat_hi, 1)
                act.wait_ge(cache_turned, l + 1)
                act.activation(HH[:, CKV:CKV + 2 * KEYS].rearrange("p (k c) -> p k c", k=2)[:, :, T:KEYS],
                               by(PS[:, 3 * BANK:3 * BANK + 2048], 2), ACT.Copy).then_inc(cache_hi, 1)
                act.wait_ge(kr_full, l + 1)
                act.activation(KH[0][64:96], KF[64:96, 0:SEQ], ACT.Copy)
                act.activation(KH[1][64:96], KF[64:96, 0:SEQ], ACT.Copy).then_inc(krope_hi, 1)

                def natural_rows():
                    for c in range(CH):
                        w = P if c < CH - 1 else DEC
                        st = CACHE + c * 288
                        act.wait_ge(nat_turned, l * CH + c + 1)
                        act.activation(Y[0:w, st:st + 288], bank(3 + c % 5, 288, (0, w)), ACT.Copy).then_inc(nat_staged, 1)
                    act.wait_ge(nat_staged, (l + 1) * CH)
                    rows = Y[:, CACHE:CACHE + (CH - 1) * 288].rearrange("p (c e) -> p c e", c=CH - 1)
                    last = CACHE + (CH - 1) * 288
                    act.dma_start(o["new_ckv_prompt"][one, 0, :, :].rearrange("l (c t) e -> t (l c) e", t=P), rows[:, :, 0:RANK]).then_inc(nat_stored, 16)
                    act.dma_start(o["new_krope_prompt"][one, 0, :, :].rearrange("l (c t) e -> t (l c) e", t=P), rows[:, :, RANK:288]).then_inc(nat_stored, 16)
                    act.dma_start(o["new_ckv_sample"][one, 0, :, :].rearrange("l t c -> (l t) c"), Y[0:DEC, last:last + RANK]).then_inc(nat_stored, 16)
                    act.dma_start(o["new_krope_sample"][one, 0, :, :].rearrange("l t c -> (l t) c"), Y[0:DEC, last + RANK:last + 288]).then_inc(nat_stored, 16)

                def prepare(p, h, stage):
                    hd = (l * PAIRS + p) * 2 + h
                    if stage == "q":
                        act.wait_ge(q_proj, hd + 1)
                        act.wait_ge(q_split, hd)
                        act.activation(by(X[0:64, QF:QF + T], 3), pset(0, (0, 64)), ACT.Copy).then_inc(qnope_ready, 1)
                        act.wait_ge(qf_ready, hd + 1)
                        act.activation(QH[h][0:96], X[0:96, QF:QF + SEQ], ACT.Copy).then_inc(qhi_ready, 1)
                    elif stage in ("kv0", "kv1"):
                        r = int(stage[2])
                        n = 3 - r
                        act.wait_ge(kv_proj, hd * 2 + r + 1)
                        act.activation(by(X[64:128, VTF + r * 1248:VTF + r * 1248 + n * 416], n),
                                       by(PS[64:128, 0:n * BANK], n)[:, :, 0:416], ACT.Copy).then_inc(vt_ready, 1)
                        if r == 0:
                            act.wait_ge(kf_ready, hd * 2 + 1)
                            act.activation(KH[h][0:64], KF[0:64, 0:SEQ], ACT.Copy).then_inc(khi_ready, 1)
                    elif stage == "sample":
                        act.wait_ge(ss_max, hd + 1)
                        act.activation(by(SS[0:DEC, :], 3), pset(0, (0, DEC)), ACT.Exp, bias=SMALL[0:DEC, 21:22], scale=SCALE,
                                       accum_out=SMALL[0:DEC, 22:23]).then_inc(ss_exp, 1)
                    elif stage == "mrow":
                        act.wait_ge(mrow_turned, hd + 1)
                        act.activation(QH[h][96:97], PS[0:1, BANK:BANK + SEQ], ACT.Copy, scale=-1.0).then_inc(mrow_ready, 1)

                def finish(p, h):
                    act.wait_ge(pv_done, ((l * PAIRS + p) * 2 + h + 1) * NB)
                    act.activation(W2[0:64, 0:SEQ], PS[64:128, 6 * BANK:8 * BANK], ACT.Ln)
                    act.drain()
                    act.activation(W2[0:64, 0:SEQ], W2[0:64, 0:SEQ], ACT.Exp, scale=-1.0).then_inc(rden_ready, 1)

                def attend(p, h, np, nh):
                    hd = (l * PAIRS + p) * 2 + h
                    for b in range(NB + 2):
                        if b < NB:
                            kt, q0, q1 = BLOCKS[b]
                            w = q1 - q0
                            act.wait_ge(s_ready, hd * NB + b + 1)
                            if b >= 2:
                                act.wait_ge(p_ready, hd * NB + b - 1)
                            f = slice(PF + b % 2 * BANK, PF + b % 2 * BANK + w)
                            act.activation(X[:, f], bank(3 + b % 3, w), ACT.Exp, scale=SCALE).then_inc(p_exp, 1)
                            act.drain()
                            if b >= 2:
                                act.wait_ge(pv_done, hd * NB + b - 1)
                            act.activation(RH[:, PO + b % 2 * BANK:PO + b % 2 * BANK + w], X[:, f], ACT.Copy).then_inc(p_hi, 1)
                            if b == 0:
                                if h == 1:
                                    finish(p, 0)
                                elif not isinstance(p, int):
                                    finish(p - 1, 1)
                                act.wait_ge(v_staged, hd + 1)
                                act.activation(RH[:, VO:VO + SEQ].rearrange("p (t c) -> p t c", t=8)[:, :, 0:HD],
                                               by(X[:, VS:VS + 8 * HD], 8), ACT.Copy).then_inc(vhi_ready, 1)
                        if np is not None:
                            for stage in PREPARE.get(b, ()):
                                prepare(np, nh, stage)

                act.preload_act_table_set("natural_log_exp_and_others")
                prepare(0, 0, "q")
                natural_rows()
                for stage in STAGES[1:]:
                    prepare(0, 0, stage)
                act.wait_ge(rows_set, l + 1)
                attend(0, 0, 0, 1)
                with act.Fori(0, PAIRS - 1) as p:
                    attend(p, 1, p + 1, 0)
                    attend(p + 1, 0, p + 1, 1)
                attend(PAIRS - 1, 1, None, None)
                finish(PAIRS - 1, 1)

                act.wait_ge(attn_out, (l + 1) * HEADS + 1)
                act.wait_ge(prompt_out, (l + 1) * HEADS)
                act.dma_start(X[:, :], x_spill).then_inc(x_back, 16)
                for k in range(KT):
                    act.activation(HH[:, k * T:(k + 1) * T], yt(k), ACT.Copy).then_inc(mix_hi, 1)
                with act.Fori(0, KT // 2) as m:
                    for i in range(2):
                        act.wait_ge(emptied[i], l * SET_USES[i] + SET_OUT[i] + m + 2)
                        act.wait_ge(sq_added, l * SUMS + SUMS_OF[1] + 2 * m + i - 1)
                        square(l, 1, i, Y[:, bass.ds((2 * m + i) * T, T)])
                rstd(l, 3, D)
                squares_of_x(l, 2, mid_ready)
                rstd(l, 4, D)
                hi_of_h(l, 1)

                act.wait_ge(tile_done, l * TILES + TILE_FFN + 1)
                act.activation(by(W2[:, 0:T], 3), pset(0), ACT.Silu).then_inc(emptied[0], 1)
                with act.Fori(0, FG - 1) as g:
                    base = l * TILES + TILE_FFN + 12 * g
                    act.wait_ge(tile_done, base + 3)
                    act.wait_ge(ff_ready, (l * FG + g) * 2 + 1)
                    act.activation(by(W2[:, T:2 * T], 3), pset(0), ACT.Silu).then_inc(emptied[0], 1)
                    act.wait_ge(tile_done, base + 5)
                    act.activation(by(W2[:, 0:T], 3), pset(0), ACT.Silu).then_inc(emptied[0], 1)
                act.wait_ge(tile_done, l * TILES + TILE_FFN + 12 * (FG - 1) + 3)
                act.wait_ge(ff_ready, (l * FG + FG - 1) * 2 + 1)
                act.activation(by(W2[:, T:2 * T], 3), pset(0), ACT.Silu).then_inc(emptied[0], 1)
                act.preload_act_table_set("natural_log_exp_and_others")
                for m in range(KT):
                    s = m % 2
                    act.wait_ge(emptied[s], (l + 1) * SET_USES[s] + 1 - (KT // 2 - 1 - m // 2))
                    act.wait_ge(sq_added, l * SUMS + SUMS_OF[3] + max(m - 1, 0))
                    square(l, 3, m, yt(m))
                rstd(l, 5, D)

            for c in range(CH):
                act.wait_ge(out_staged, c + 1)
                if c < CH - 1:
                    act.dma_start(o["y_prompt"][0, c * P:(c + 1) * P, :], Y[:, c * D:(c + 1) * D]).then_inc(out_stored, 16)
                else:
                    act.dma_start(o["y_sample"][0, :, :], W2[0:DEC, 0:D]).then_inc(out_stored, 16)
            act.wait_ge(out_stored, 16 * CH)
            act.wait_ge(m_stored, 32 * LAYERS)
            act.wait_ge(state_stored, 16 + 128 * PAIRS * LAYERS)
            act.wait_ge(nat_stored, 64 * LAYERS)

        @block.vector
        def _(dve):
            def add_square(l, i, k, n):
                dve.drain()
                dve.wait_ge(sq_ready, (l * 4 + i) * KT + k + 1)
                dve.tensor_tensor(SS[:, :], SS[:, :], W2[:, n * T:(n + 1) * T], ALU.add).then_inc(sq_added, 1)

            def normed(l, i, norm):
                dve.wait_ge(rs_ready, l * NORMS + norm + 1)
                gain = 0 if i == 0 else 2

                def lo(k):
                    if k in LO_DVE:
                        dve.wait_ge(hi_ready, l * 2 * KT + i * KT + k + 1)
                        dve.tensor_tensor(HL[:, k * T:(k + 1) * T], yt(k), HH[:, k * T:(k + 1) * T], ALU.subtract).then_inc(h_ready, 1)
                for k in range(KT):
                    dve.scalar_tensor_tensor(out=yt(k), in0=xt(k),
                                             scalar=GN[:, bass.ds((l * 4 + gain) * KT + k, 1)], in1=RS[:, :], op0=ALU.mult, op1=ALU.mult)\
                       .then_inc(scaled, 1)
                    if k >= 1:
                        lo(k - 1)
                lo(KT - 1)

            def residual(l, norm, gain, signal):
                dve.wait_ge(rs_ready, l * NORMS + norm + 1)
                for k in range(KT):
                    dve.scalar_tensor_tensor(out=yt(k), in0=yt(k), scalar=GN[:, bass.ds((l * 4 + gain) * KT + k, 1)], in1=RS[:, :],
                                             op0=ALU.mult, op1=ALU.mult)
                    dve.drain()
                    dve.tensor_tensor(xt(k), xt(k), yt(k), ALU.add).then_inc(signal, 1)

            for s in range(2):
                dve.memset(SH[:, s * SLAB:(s + 1) * SLAB].bitcast(F32), 0.0).then_inc(slab_free[s], 1)
                dve.memset(RS[:, 32 + 8 * s:40 + 8 * s], 0.0).then_inc(emptied[s], 1)
            dve.memset(RH[:, 2 * T:2 * T + SLAB].bitcast(F32), 0.0).then_inc(slab_free[2], 1)
            dve.memset(RS[:, 0:8], 0.0).then_inc(mout_done, 1)
            dve.memset(RS[:, 8:16], 0.0).then_inc(attn_out, 1)
            dve.memset(RS[:, 16:24], 0.0).then_inc(state_stored, 16)
            dve.wait_ge(const_loaded, CONSTS)
            for c in range(CH):
                w = P if c < CH - 1 else DEC
                dve.wait_ge(in_turned, c + 1)
                src = PS[:, 2 * (c % 4) * BANK:2 * (c % 4 + 1) * BANK].rearrange("p (k c) -> p k c", k=KT)[:, :, 0:w]
                dve.tensor_copy(X[:, :].rearrange("p (k c) -> p k c", k=KT)[:, :, c * P:c * P + w], src).then_inc(in_taken, 1)
            dve.drain()
            dve.memset(RS[:, 24:32], 0.0).then_inc(x_ready, KT)

            with dve.Fori(0, LAYERS) as l:
                normed(l, 0, 0)

                bias = lambda i: BG[:, bass.ds(l * 3 + i, 1)]
                g3 = lambda i: by(gt(i, 0, T), 3)
                dve.wait_ge(x_spilled, (l + 1) * 16)
                dve.wait_ge(tile_done, l * TILES + 1)
                dve.tensor_copy(by(Y[64:128, KRRAW:KRRAW + T], 3), pset(0, (64, 128)))
                dve.tensor_scalar(g3(0), pset(0, (0, 8)), bias(0), None, ALU.add)
                dve.memset(gt(0, T, TP), NEG)
                dve.tensor_copy(g3(1), pset(0, (32, 40))).then_inc(emptied[0], 1)
                dve.drain()
                dve.tensor_scalar(gt(1, 0, T), gt(1, 0, T), bias(1), None, ALU.add)
                dve.drain()
                dve.scalar_tensor_tensor(out=gt(2, 0, T), in0=gt(1, 0, T), scalar=-1.0, in1=gt(1, 0, T), op0=ALU.mult, op1=ALU.min).then_inc(f_ready, 1)
                dve.memset(gt(4), 1.0)
                dve.memset(X[:, G4:G4 + TP], 0.0)
                dve.drain()
                dve.memset(gt(4).rearrange("p (c t) -> p c t", c=CH)[:, :, 0:1], 0.0)
                dve.wait_ge(softplus_ready, l + 1)
                dve.scalar_tensor_tensor(out=gt(1, 0, T), in0=gt(1, 0, T), scalar=0.0, in1=gt(3, 0, T), op0=ALU.min, op1=ALU.subtract)
                dve.memset(gt(1, T, TP), 0.0)
                dve.drain()
                dve.tensor_tensor_scan(gt(2, 0, SEQ), gt(1, 0, SEQ), gt(0, 0, SEQ), 0.0, ALU.add, ALU.max)
                dve.tensor_tensor_scan(gt(2, SEQ, TP), gt(1, SEQ, TP), gt(0, SEQ, TP), bias(2), ALU.add, ALU.max)
                dve.tensor_tensor_scan(gt(3), gt(4), gt(1), 0.0, ALU.mult, ALU.add)
                dve.drain()
                dve.tensor_tensor(UROW[:, :], gt(3), gt(2), ALU.subtract)
                dve.tensor_copy(SMALL[0:8, 0:8], gt(2, 0, SEQ).rearrange("p (c t) -> p c t", c=8)[:, :, 127:128].rearrange("p c t -> p (c t)"))
                dve.tensor_copy(SMALL[0:8, 8:9], gt(2, T - 1, T))
                dve.tensor_copy(SMALL[0:8, 10:18], gt(3, 0, SEQ).rearrange("p (c t) -> p c t", c=8)[:, :, 127:128].rearrange("p c t -> p (c t)"))
                dve.tensor_copy(SMALL[0:8, 18:19], gt(3, T - 1, T))
                dve.memset(SMALL[0:8, 20:21], 0.0)
                dve.tensor_copy(SMALL[0:8, 28:29], bias(2))
                dve.tensor_tensor(gt(0), gt(0), gt(3), ALU.subtract)
                dve.drain()
                dve.tensor_copy(SMALL[0:8, 21:28], SMALL[0:8, 0:7])
                dve.tensor_tensor(SMALL[0:8, 10:19], SMALL[0:8, 10:19], SMALL[0:8, 0:9], ALU.subtract)
                dve.drain()
                dve.tensor_tensor(SMALL[0:8, 30:39], SMALL[0:8, 10:19], SMALL[0:8, 20:29], ALU.add)
                c9 = lambda ap: ap.rearrange("p (c t) -> p c t", c=CH)
                over = lambda ap: ap.unsqueeze(2).broadcast_to([8, CH, P])
                dve.tensor_tensor(c9(gt(1)), c9(UROW[:, :]), over(SMALL[0:8, 20:29]), ALU.add)
                dve.tensor_tensor(c9(gt(4)), c9(gt(0)), over(SMALL[0:8, 10:19]), ALU.add)
                dve.drain()
                dve.memset(SMALL[0:8, 60:61], 0.0).then_inc(args_ready, 1)
                dve.wait_ge(gate_turned, l + 1)
                dve.tensor_copy(N4[:, :].rearrange("p (c q h) -> p c q h", c=CH, q=4),
                                PS[:, 3 * BANK:3 * BANK + TP].rearrange("p (c q h) -> p c q h", c=CH, q=4)[:, :, :, 0:8])
                dve.tensor_copy(DEC_ALL[:, :], bank(6, PAIRS * CH))
                dve.drain()
                dve.memset(SMALL[0:8, 60:61], 0.0).then_inc(gates_ready, 1)
                for t in (*QTS, *KTS, VT):
                    dve.memset(t[:, T:TP], 0.0)
                dve.memset(VX, 1.0)
                dve.wait_ge(gate_turned, l + 1)
                dve.memset(CS, 0.0)
                dve.drain()
                dve.memset(SMALL[0:8, 60:61], 0.0).then_inc(mixer_cleared, 1)

                def mlstm(p, par):
                    u = l * PAIRS + p
                    ds = lambda start, n: slice(start, start + n) if isinstance(p, int) else bass.ds(start, n)

                    def per_token(q, c0, c1, inner):
                        cols = N4[:, :].rearrange("p (c j) -> p c j", c=CH)[:, c0:c1, ds(2 * p + 8 * q, 2)]
                        return cols.unsqueeze(3).broadcast_to([P, c1 - c0, 2, inner])
                    dve.wait_ge(kv_turned, u * 2 + 2)
                    kw = KW.rearrange("p (c h e) -> p c h e", c=CH, h=2)
                    dve.tensor_tensor(kw[:, 0:CH - 1], PS[:, 5 * BANK:7 * BANK].rearrange("p (c h e) -> p c h e", c=CH - 1, h=2),
                                      per_token(1, 0, CH - 1, HD), ALU.mult)
                    dve.wait_ge(vx_ready, u + 1)
                    dve.tensor_tensor(kw[:, CH - 1:CH], bank(7, P, off=P).rearrange("p (c h e) -> p c h e", c=1, h=2),
                                      per_token(1, CH - 1, CH, HD), ALU.mult).then_inc(kw_ready, 1)

                    def u_rows(g):
                        for h in range(2):
                            m = dve.tensor_scalar(UM[0:8, h * 384:(h + 1) * 384], UROW[:, g * 384:(g + 1) * 384],
                                                  IDN[0:8, ds(2 * p + h, 1)], None, ALU.mult)
                        m.then_inc(um_ready, 1)

                    def exponents(g):
                        dve.wait_ge(u_ready, u * 3 + g + 1)
                        dve.tensor_tensor(PTG[g % 2].rearrange("p (h c t) -> p h c t", h=2, c=3),
                                          PS[:, 3 * BANK:5 * BANK].rearrange("p (h r) -> p h r", h=2)[:, :, 0:384].rearrange("p h (c t) -> p h c t", c=3),
                                          CM[:, :].unsqueeze(1).unsqueeze(1).broadcast_to([P, 2, 3, P]), ALU.add).then_inc(dm_ready, 1)
                    u_rows(0)
                    dve.wait_ge(upd_ready, u + 1)
                    dve.wait_ge(state_stored, u * 128 + 16)
                    dve.tensor_tensor(X[:, C0 + 2 * HB:C0 + 10 * 2 * HB].rearrange("p (g c e) -> p g c e", g=3, c=3),
                                      PS[:, 3 * BANK:6 * BANK].rearrange("p (g r) -> p g r", g=3)[:, :, 0:6 * HB].rearrange("p g (c e) -> p g c e", c=3),
                                      BM[:, :].unsqueeze(1).unsqueeze(1).broadcast_to([P, 3, 3, 2 * HB]), ALU.mult).then_inc(states_ready, 1)

                    def chain(c0, c1):
                        for c in range(c0, c1):
                            src, dst = (c, c + 1) if c < CH - 1 else (10, 9)
                            dve.drain()
                            if c == CH - 1:
                                dve.wait_ge(state_loaded, (u + 1) * 64)
                            dve.scalar_tensor_tensor(out=cs(dst), in0=cs(src), scalar=DEC_ALL[:, ds(p * CH + c, 1)], in1=cs(dst),
                                                     op0=ALU.mult, op1=ALU.add)
                        dve.drain()
                    exponents(0)
                    chain(1, CH)
                    for g in range(3):
                        n = u * 3 + g
                        if g < 2:
                            u_rows(g + 1)
                        dve.wait_ge(st_ready, n + 1)
                        dve.wait_ge(pt_ready, n + 1)
                        dve.tensor_tensor(by(WT, 2), PS[:, 5 * BANK:7 * BANK].rearrange("p (h r) -> p h r", h=2)[:, :, 0:384], by(PTG[g % 2], 2), ALU.mult)\
                           .then_inc(w_ready, 1)
                        if g < 2:
                            exponents(g + 1)
                        dve.wait_ge(num_ready, n + 1)
                        c6 = lambda ap: ap.rearrange("p (c h e) -> p c h e", c=3, h=2)
                        dve.tensor_tensor(c6(T1), c6(bank(5, 6 * HB)), per_token(0, g * CG, g * CG + 3, HB), ALU.mult)
                        dve.drain()
                        dve.tensor_tensor(T1, bank(7, 6 * HB), T1, ALU.add)
                        dve.drain()
                        den = c6(T1)[:, :, :, HD:HB].rearrange("p c h e -> p c (h e)")
                        r6 = SMALL[:, 32:38].rearrange("p (c h) -> p c h", c=3)
                        dve.scalar_tensor_tensor(out=r6, in0=den, scalar=-1.0, in1=den, op0=ALU.mult, op1=ALU.max)
                        dve.drain()
                        em = N4[:, :].rearrange("p (c j) -> p c j", c=CH)[:, g * CG:g * CG + 3, ds(2 * p + 16, 2)]
                        dve.tensor_tensor(r6, r6, em, ALU.max)
                        dve.drain()
                        dve.reciprocal(SMALL[:, 32:38], SMALL[:, 32:38])
                        dve.drain()
                        wide = lambda ap: ap.rearrange("p (c h) -> p c h", c=3).unsqueeze(3).broadcast_to([P, 3, 2, HD])
                        dve.tensor_tensor(c6(HBUF), c6(T1)[:, :, :, 0:HD], wide(SMALL[:, 32:38]), ALU.mult)
                        dve.drain()
                        dve.tensor_tensor(SQ, HBUF, HBUF, ALU.mult)
                        dve.drain()
                        dve.tensor_reduce(SMALL[:, 48:54], SQ.rearrange("p (c e) -> p c e", c=6), AX, ALU.add).then_inc(ms_head, 1)
                        dve.wait_ge(rr_ready, n + 1)
                        dve.tensor_tensor(c6(HBUF), c6(HBUF), wide(SMALL[:, 48:54]), ALU.mult).then_inc(hn_ready, 1)
                        dve.wait_ge(ht_ready, n + 1)
                        w = 384 if g < 2 else 256 + DEC
                        dve.scalar_tensor_tensor(out=Y[:, ds(p * T + g * 384, w)], in0=bank(6, w), scalar=GM[:, bass.ds(l * PAIRS + p, 1)],
                                                 in1=OMS[par][:, g * 384:g * 384 + w], op0=ALU.mult, op1=ALU.mult).then_inc(mout_done, 1)
                mlstm(0, 0)
                with dve.Fori(0, PAIRS // 2 - 1) as i:
                    mlstm(2 * i + 1, 1)
                    mlstm(2 * i + 2, 0)
                mlstm(PAIRS - 1, 1)

                for i in range(2):
                    dve.wait_ge(csq_ready, l * 4 + 2 * i + 2)
                    dve.tensor_tensor(LSUM[i][:, 0:T], LSQ[i][0], LSQ[i][1], ALU.add).then_inc(csq_added, 1)

                def scale_latent(i):
                    dve.wait_ge(rs_ready, l * NORMS + 2 + i)
                    for j in range(2):
                        t = X[:, (2 * i + j) * T:(2 * i + j + 1) * T]
                        dve.scalar_tensor_tensor(out=t, in0=t, scalar=GC[:, bass.ds(l * 4 + 2 * i + j, 1)], in1=LRS[i][:, 0:T],
                                                 op0=ALU.mult, op1=ALU.mult).then_inc(lat_scaled, 1)

                def latent_lo(i):
                    for j in range(2):
                        dst = CQ + j * T if i == 0 else CKV + j * KEYS
                        dve.wait_ge(lat_hi, l * 4 + 2 * i + j + 1)
                        dve.tensor_tensor(HL[:, dst:dst + T], X[:, (2 * i + j) * T:(2 * i + j + 1) * T], HH[:, dst:dst + T], ALU.subtract)\
                            .then_inc(lat_ready, 1)
                scale_latent(0)
                latent_lo(0)
                dve.wait_ge(state_stored, (l + 1) * PAIRS * 128 + 16)
                dve.wait_ge(kr_mul, l + 1)
                dve.tensor_tensor(X[64:96, KRF:KRF + T], W2[64:96, T:2 * T], W2[96:128, T:2 * T], ALU.add)
                scale_latent(1)
                dve.wait_ge(kr_turned, l + 1)
                dve.tensor_copy(X[64:96, KRF + T:KRF + KEYS], PS[0:ROPE, 0:PAST])
                dve.drain()
                dve.memset(SMALL[0:8, 60:61], 0.0).then_inc(kr_full, 1)
                latent_lo(1)
                dve.wait_ge(cache_hi, l + 1)
                tail = lambda t: t[:, CKV:CKV + 2 * KEYS].rearrange("p (k c) -> p k c", k=2)[:, :, T:KEYS]
                dve.tensor_tensor(tail(HL), by(PS[:, 3 * BANK:3 * BANK + 2048], 2), tail(HH), ALU.subtract).then_inc(cache_lo, 1)

                def key_constants():
                    dve.wait_ge(krope_hi, l + 1)
                    for i in range(2):
                        k = dve.tensor_tensor(KL[i][64:96], KF[64:96, 0:SEQ], KH[i][64:96], ALU.subtract)
                    k.then_inc(keys_ready, 1)

                def prepare(p, h, stage):
                    hd = (l * PAIRS + p) * 2 + h
                    if stage == "q":
                        dve.wait_ge(q_proj, hd + 1)
                        dve.tensor_tensor(by(W2[64:128, T:2 * T], 3), pset(0, (64, 128)), by(X[64:128, TRIG:TRIG + T], 3), ALU.mult)
                        dve.drain()
                        dve.wait_ge(q_split, hd)
                        dve.wait_ge(qnope_ready, hd + 1)
                        dve.tensor_tensor(X[64:96, QF:QF + T], W2[64:96, T:2 * T], W2[96:128, T:2 * T], ALU.add).then_inc(qf_ready, 1)
                    elif stage in ("kv0", "kv1"):
                        r = int(stage[2])
                        n = 3 - r
                        dve.wait_ge(kv_proj, hd * 2 + r + 1)
                        if r == 0:
                            dve.wait_ge(k_split, hd)
                        dve.tensor_copy(by(KF[0:64, r * 1248:r * 1248 + n * 416], n), by(PS[0:64, 0:n * BANK], n)[:, :, 0:416]).then_inc(kf_ready, 1)
                    elif stage == "v":
                        dve.wait_ge(v_turned, hd + 1)
                        dve.wait_ge(vhi_ready, hd)
                        dve.tensor_copy(X[:, VS:VS + 16 * HD], PS[:, 0:16 * HD])
                        dve.tensor_copy(X[0:DEC, VS + 16 * HD:VS + 17 * HD], PS[0:DEC, 16 * HD:17 * HD]).then_inc(v_staged, 1)
                    elif stage == "sample":
                        dve.wait_ge(ss_scores, hd + 1)
                        dve.tensor_reduce(SMALL[0:DEC, 20:21], PS[0:DEC, 0:3 * BANK].rearrange("p (n c) -> p n c", n=3)[:, :, 0:TG], mybir.AxisListType.XY, ALU.max)
                        dve.drain()
                        dve.tensor_scalar(SMALL[0:DEC, 21:22], SMALL[0:DEC, 20:21], -SCALE, None, ALU.mult).then_inc(ss_max, 1)
                    elif stage[:3] == "max":
                        if stage == "max0":
                            dve.wait_ge(ss_exp, hd + 1)
                            dve.reciprocal(SMALL[0:DEC, 23:24], SMALL[0:DEC, 22:23])
                            dve.drain()
                            dve.tensor_scalar(SS[0:DEC, :], SS[0:DEC, :], SMALL[0:DEC, 23:24], None, ALU.mult).then_inc(ss_probs, 1)
                        for j in range(3 * int(stage[3]), 3 * int(stage[3]) + 3):
                            i, k0, k1 = MAX_BLOCKS[j]
                            w, base = k1 - k0, (j % 3) * BANK
                            col = i if k0 == 0 else 30 + i - 4
                            dve.wait_ge(smax_ready, hd * NM + j + 1)
                            if k1 == (i + 1) * P:
                                dve.tensor_reduce(SMALL[64:128, 10 + i:11 + i], PS[64:128, base + w - 64:base + w], AX, ALU.max)
                                w -= 64
                            dve.tensor_reduce(SMALL[:, col:col + 1], PS[:, base:base + w], AX, ALU.max).then_inc(smax_taken, 1)
                        if stage == "max3":
                            dve.drain()
                            dve.tensor_tensor(SMALL[:, 4:8], SMALL[:, 4:8], SMALL[:, 30:34], ALU.max)
                            dve.drain()
                            dve.tensor_tensor(SMALL[64:128, 0:8], SMALL[64:128, 0:8], SMALL[64:128, 10:18], ALU.max).then_inc(max_ready, 1)
                    elif stage == "turn":
                        dve.wait_ge(ss_turned, hd + 1)
                        dve.tensor_copy(PTS[:, 0:8 * DEC], bank(0, 8 * DEC))
                        dve.tensor_copy(PTS[0:DEC, 8 * DEC:9 * DEC], bank(0, DEC, (0, DEC), 8 * DEC)).then_inc(ss_pt, 1)
                    elif stage == "out":
                        dve.wait_ge(ss_pv, hd + 1)
                        dve.tensor_copy(Y[64 * h:64 * h + 64, bass.ds((4 + p) * T + SEQ, DEC)], bank(0, DEC, (0, HD), 9 * DEC)).then_inc(attn_out, 1)

                def finish(p, h):
                    dve.wait_ge(rden_ready, (l * PAIRS + p) * 2 + h + 1)
                    col = (4 + p) * T
                    out = Y[64 * h:64 * h + 64, col:col + SEQ] if isinstance(p, int) else Y[64 * h:64 * h + 64, bass.ds(col, SEQ)]
                    dve.tensor_tensor(out, PS[0:64, 6 * BANK:8 * BANK], W2[0:64, 0:SEQ], ALU.mult).then_inc(prompt_out, 1)

                def attend(p, h, np, nh):
                    hd = (l * PAIRS + p) * 2 + h
                    v8 = lambda t: t[:, VO:VO + SEQ].rearrange("p (t c) -> p t c", t=8)[:, :, 0:HD]
                    for b in range(NB + 2):
                        if b < NB:
                            kt, q0, q1 = BLOCKS[b]
                            w = q1 - q0
                            f = slice(PF + b % 2 * BANK, PF + b % 2 * BANK + w)
                            r = slice(PO + b % 2 * BANK, PO + b % 2 * BANK + w)
                            dve.wait_ge(p_hi, hd * NB + b + 1)
                            if q0 == kt * P:
                                dve.memset(X[64:128, f.start:f.start + 64], 0.0)
                                dve.memset(RH[64:128, r.start:r.start + 64].bitcast(F32), 0.0)
                                dve.drain()
                            dve.tensor_tensor(RL[:, r], X[:, f], RH[:, r], ALU.subtract).then_inc(p_ready, 1)
                            if b == 0:
                                if h == 1:
                                    finish(p, 0)
                                elif not isinstance(p, int):
                                    finish(p - 1, 1)
                                dve.wait_ge(vhi_ready, hd + 1)
                                dve.tensor_tensor(v8(RL), by(X[:, VS:VS + 8 * HD], 8), v8(RH), ALU.subtract).then_inc(v_ready, 1)
                        if np is not None:
                            for stage in PREPARE.get(b, ()):
                                prepare(np, nh, stage)
                prepare(0, 0, "q")
                key_constants()
                for stage in STAGES[1:]:
                    if stage == "out":
                        dve.wait_ge(nat_stored, (l + 1) * 64)
                    prepare(0, 0, stage)
                dve.wait_ge(rows_set, l + 1)
                attend(0, 0, 0, 1)
                with dve.Fori(0, PAIRS - 1) as p:
                    attend(p, 1, p + 1, 0)
                    attend(p + 1, 0, p + 1, 1)
                attend(PAIRS - 1, 1, None, None)
                finish(PAIRS - 1, 1)

                for k in range(KT):
                    dve.wait_ge(mix_hi, l * KT + k + 1)
                    dve.tensor_tensor(HL[:, k * T:(k + 1) * T], yt(k), HH[:, k * T:(k + 1) * T], ALU.subtract).then_inc(mix_ready, 1)
                dve.memset(SS[:, :], 0.0)
                dve.drain()
                with dve.Fori(0, KT // 2) as m:
                    for i in range(2):
                        dve.wait_ge(tile_done, l * TILES + TILE_OUT + 2 * m + i + 1)
                        dve.tensor_copy(by(Y[:, bass.ds((2 * m + i) * T, T)], 3), pset(i)).then_inc(emptied[i], 1)
                        add_square(l, 1, 2 * m + i, i)
                dve.wait_ge(x_back, (l + 1) * 16)
                residual(l, 3, 1, mid_ready)
                dve.drain()
                normed(l, 1, 4)

                dve.drain()
                dve.wait_ge(h_ready_pool, (l + 1) * 2 * len(LO_POOL))
                dve.memset(Y[:, :], 0.0)
                dve.memset(SS[:, :], 0.0)

                def inner(g, j, tile, gate_emptied):
                    w, f = slice(j * T, (j + 1) * T), slice(j * T, (j + 1) * T)
                    dve.wait_ge(tile_done, tile + 1)
                    dve.wait_ge(emptied[0], gate_emptied)
                    dve.tensor_tensor(by(W2[:, w], 3), pset(1), by(W2[:, w], 3), ALU.mult).then_inc(emptied[1], 1)
                    dve.drain()
                    dve.tensor_copy(RH[:, f], W2[:, w])
                    dve.drain()
                    dve.tensor_tensor(RL[:, f], W2[:, w], RH[:, f], ALU.subtract).then_inc(ff_ready, 1)

                def outer(tile, s0, last=False):
                    for m in range(KT):
                        s = (s0 + m) % 2
                        dve.wait_ge(tile_done, tile + m + 1)
                        dve.tensor_tensor(by(yt(m), 3), pset(s), by(yt(m), 3), ALU.add).then_inc(emptied[s], 1)
                        if last and m >= 1:
                            add_square(l, 3, m - 1, (m - 1) % 2)
                base0 = l * SET_USES[0] + SET_FFN[0] + 1
                with dve.Fori(0, FG - 1) as g:
                    tile = l * TILES + TILE_FFN + 12 * g
                    inner(g, 0, tile + 1, base0 + 6 * g + 1)
                    inner(g, 1, tile + 3, base0 + 6 * g + 2)
                    outer(tile + 5, 1)
                tile = l * TILES + TILE_FFN + 12 * (FG - 1)
                inner(FG - 1, 0, tile + 1, base0 + 6 * (FG - 1) + 1)
                inner(FG - 1, 1, tile + 3, base0 + 6 * (FG - 1) + 2)
                outer(tile + 4, 0, last=True)
                dve.drain()
                add_square(l, 3, KT - 1, 1)
                residual(l, 5, 3, x_ready)
                dve.drain()

            for c in range(CH):
                w = P if c < CH - 1 else DEC
                dve.wait_ge(out_turned, c + 1)
                src = PS[0:w, 2 * (c % 4) * BANK:2 * (c % 4 + 1) * BANK]
                dst = Y[:, c * D:(c + 1) * D] if c < CH - 1 else W2[0:DEC, 0:D]
                dve.tensor_copy(dst, src).then_inc(out_staged, 1)


_INS = ['x_prompt', 'x_sample', 'cache_ckv', 'cache_krope', 'state_mlstm_C', 'state_mlstm_n', 'state_mlstm_m',
        'g_pre_mix', 'g_post_mix', 'g_pre_ffn', 'g_post_ffn', 'w_in', 'b_gates', 'g_mlstm_head',
        'g_q_norm', 'w_uq', 'g_kv_norm', 'w_ukv', 'w_out', 'w_ffn_in', 'w_ffn_out']
_OUTS = [('y_prompt', (1, SEQ, D)), ('y_sample', (1, DEC, D)),
         ('new_ckv_prompt', (LAYERS, 1, SEQ, RANK)), ('new_krope_prompt', (LAYERS, 1, SEQ, ROPE)),
         ('C_prompt', (LAYERS, 1, HEADS, HD, HD)), ('n_prompt', (LAYERS, 1, HEADS, HD)), ('m_prompt', (LAYERS, 1, HEADS)),
         ('new_ckv_sample', (LAYERS, 1, DEC, RANK)), ('new_krope_sample', (LAYERS, 1, DEC, ROPE)),
         ('C_sample', (LAYERS, 1, HEADS, HD, HD)), ('n_sample', (LAYERS, 1, HEADS, HD)), ('m_sample', (LAYERS, 1, HEADS))]


def shape_constants():
    import numpy as np
    t = np.arange(P)
    half = ROPE // 2
    inv = (np.float32(10000.0) ** (-np.arange(half, dtype=np.float32) / np.float32(half))).astype(np.float32)
    ang = (np.arange(T, dtype=np.float32)[None, :] * inv[:, None]).astype(np.float32)
    cos, sin = np.cos(ang), np.sin(ang)
    pair_mask = np.zeros((P, 2 * HB), np.float32)
    pair_mask[:64, :HB] = 1
    pair_mask[64:, HB:] = 1
    select = np.zeros((8, PAIRS, P), np.float32)
    for j in range(PAIRS):
        select[2 * j, j, :64] = 1
        select[2 * j + 1, j, 64:] = 1
    return {
        "identity": np.eye(P, dtype=np.float32),
        "causal": np.where(t[:, None] <= t[None, :], np.float32(0), np.float32(NEG)).astype(np.float32),
        "pair_mask": pair_mask,
        "pair_select": select.reshape(8, PAIRS * P),
        "constants": np.tile(np.array([[EPS, 1.0]], np.float32), (P, 1)),
        "ones": np.ones((P, P), np.float32),
        "zeros": np.zeros((P, 64), np.float32),
        "trig": np.concatenate([cos, cos, -sin, sin], axis=0).astype(np.float32),
    }


def kernel(**inputs):
    import numpy as _np
    import concourse.bacc as _bacc
    from concourse.bass_utils import run_bass_kernel_spmd as _run

    nc = _bacc.Bacc("TRN2", target_bir_lowering=False, num_devices=1)
    arrays, a, o = {}, {}, {}
    for name, value in [(n, inputs[n]) for n in _INS] + list(shape_constants().items()):
        v = _np.ascontiguousarray(value)
        arrays[f"in_{name}"] = v
        a[name] = nc.dram_tensor(f"in_{name}", v.shape, mybir.dt.from_np(v.dtype), kind="ExternalInput").ap()
    for name, shape in _OUTS:
        o[name] = nc.dram_tensor(f"out_{name}", shape, F32, kind="ExternalOutput").ap()
    encoder_step(nc, a, o)
    r = _run(nc, [arrays], core_ids=[0])
    return tuple(r.results[0][f"out_{name}"] for name, _ in _OUTS)
```
